# Optimizing a Trainium2 kernel written in Bass

```python
import jax, jax.numpy as jnp
from jax import lax
import numpy as np

D_MODEL = 1024
BATCH = 1
SEQ = 512
DEPTH = 1

POOL_WINDOWS = (2, 4, 8, 16)
N_POOL_GROUPS = len(POOL_WINDOWS)
POOL_WIDTH = D_MODEL
POOL_GROUP = POOL_WIDTH // N_POOL_GROUPS
HEAD_DIM = 64
N_Q_HEADS = D_MODEL // HEAD_DIM
N_KV_HEADS = 2
GQA_GROUP = N_Q_HEADS // N_KV_HEADS
WINDOW = 128
BLOCK = 128
ROPE_DIM = HEAD_DIM // 4
ROPE_THETA = 500000.0
Q_WIDTH = N_Q_HEADS * HEAD_DIM
KV_WIDTH = N_KV_HEADS * HEAD_DIM
D_FF = 2816
CONV_WIDTH = 3
EPS = 1e-6
IN_WIDTH = POOL_WIDTH + Q_WIDTH + 2 * KV_WIDTH + 2 * D_MODEL


def rmsnorm(x, g):
    xf = x.astype(jnp.float32)
    r = lax.rsqrt(jnp.mean(xf * xf, axis=-1, keepdims=True) + EPS)
    return (xf * r * g.astype(jnp.float32)).astype(x.dtype)

def partial_rope(x, positions):
    half = ROPE_DIM // 2
    inv_freq = ROPE_THETA ** (-jnp.arange(0, ROPE_DIM, 2, dtype=jnp.float32) / ROPE_DIM)
    ang = positions.astype(jnp.float32)[..., None] * inv_freq
    cos = jnp.cos(ang)[:, :, None, :]
    sin = jnp.sin(ang)[:, :, None, :]
    xf = x.astype(jnp.float32)
    x1, x2, xp = xf[..., :half], xf[..., half:ROPE_DIM], xf[..., ROPE_DIM:]
    out = jnp.concatenate([x1 * cos - x2 * sin, x2 * cos + x1 * sin, xp], axis=-1)
    return out.astype(x.dtype)

def pool_mixer(u, w_pool, pool_scale):
    B, S, _ = u.shape
    ug = u.reshape(B, S, N_POOL_GROUPS, POOL_GROUP).astype(jnp.float32)
    cs = jnp.cumsum(ug, axis=1)
    t = jnp.arange(S, dtype=jnp.float32)
    pooled = []
    for g, w in enumerate(POOL_WINDOWS):
        csg = cs[:, :, g]
        shifted = jnp.pad(csg, ((0, 0), (w, 0), (0, 0)))[:, :S]
        count = jnp.minimum(t + 1.0, float(w))[None, :, None]
        pooled.append((csg - shifted) / count)
    pooled = jnp.stack(pooled, axis=2) - ug
    mixed = jnp.einsum('bsgc,gcd->bsgd', pooled.astype(u.dtype), w_pool)
    return mixed.reshape(B, S, POOL_WIDTH) * pool_scale

def swa_sink_attention(q, k, v, sinks):
    B, S = q.shape[0], q.shape[1]
    nb = S // BLOCK
    qb = q.reshape(B, nb, BLOCK, N_KV_HEADS, GQA_GROUP, HEAD_DIM)

    def band(t):
        tb = t.reshape(B, nb, BLOCK, N_KV_HEADS, HEAD_DIM)
        prev = jnp.pad(tb, ((0, 0), (1, 0), (0, 0), (0, 0), (0, 0)))[:, :-1]
        return jnp.concatenate([prev, tb], axis=2)

    kb, vb = band(k), band(v)
    s = jnp.einsum('bnqhgd,bnkhd->bhgnqk', qb, kb,
                   preferred_element_type=jnp.float32)
    q_pos = jnp.arange(BLOCK)[:, None] + BLOCK
    k_pos = jnp.arange(2 * BLOCK)[None, :]
    rel_ok = (k_pos <= q_pos) & (q_pos - k_pos < WINDOW)
    blk_ok = (jnp.arange(nb)[:, None, None] > 0) | (k_pos[None] >= BLOCK)
    mask = rel_ok[None] & blk_ok
    s = jnp.where(mask, s, -jnp.inf)
    sink = sinks.astype(jnp.float32).reshape(1, N_KV_HEADS, GQA_GROUP, 1, 1, 1)
    m = jnp.maximum(jnp.max(s, axis=-1, keepdims=True), sink)
    p = jnp.exp(s - m)
    denom = jnp.sum(p, axis=-1, keepdims=True) + jnp.exp(sink - m)
    probs = (p / denom).astype(v.dtype)
    out = jnp.einsum('bhgnqk,bnkhd->bnqhgd', probs, vb)
    return out.reshape(B, S, Q_WIDTH)

def causal_depthwise_conv(u, w, b):
    S = u.shape[1]
    up = jnp.pad(u, ((0, 0), (CONV_WIDTH - 1, 0), (0, 0)))
    y = b
    for j in range(CONV_WIDTH):
        y = y + w[j] * up[:, j:j + S]
    return y

def first_inputs(seed: int = 0) -> dict:
    key = jax.random.key(seed)
    ks = jax.random.split(key, 18)
    f32 = jnp.float32
    nrm = lambda k, shape, s: jax.random.normal(k, shape, f32) * s
    x = jax.random.normal(ks[0], (BATCH, SEQ, D_MODEL), f32)
    offsets = jax.random.randint(ks[1], (BATCH, 1), 0, 1024, dtype=jnp.int32)
    positions = offsets + jnp.arange(SEQ, dtype=jnp.int32)[None, :]
    return {
        "x": x,
        "positions": positions,
        "attn_norm": 1.0 + nrm(ks[2], (DEPTH, D_MODEL), 0.05),
        "w_in": nrm(ks[3], (DEPTH, D_MODEL, IN_WIDTH), D_MODEL ** -0.5),
        "b_gate": nrm(ks[4], (DEPTH, 2 * D_MODEL), 0.1),
        "w_pool": nrm(ks[5], (DEPTH, N_POOL_GROUPS, POOL_GROUP, POOL_GROUP), POOL_GROUP ** -0.5),
        "pool_scale": 1.0 + nrm(ks[6], (DEPTH, POOL_WIDTH), 0.1),
        "q_norm": 1.0 + nrm(ks[7], (DEPTH, HEAD_DIM), 0.05),
        "k_norm": 1.0 + nrm(ks[8], (DEPTH, HEAD_DIM), 0.05),
        "sinks": nrm(ks[9], (DEPTH, N_Q_HEADS), 0.5),
        "w_out": nrm(ks[10], (DEPTH, D_MODEL, D_MODEL), D_MODEL ** -0.5),
        "ffn_norm": 1.0 + nrm(ks[11], (DEPTH, D_MODEL), 0.05),
        "w_up": nrm(ks[12], (DEPTH, D_MODEL, 2 * D_FF), D_MODEL ** -0.5),
        "conv_w": nrm(ks[13], (DEPTH, CONV_WIDTH, 2 * D_FF), CONV_WIDTH ** -0.5),
        "conv_b": nrm(ks[14], (DEPTH, 2 * D_FF), 0.02),
        "w_down": nrm(ks[15], (DEPTH, D_FF, D_MODEL), D_FF ** -0.5),
    }

def first_block(x, positions, attn_norm, w_in, b_gate, w_pool, pool_scale, q_norm, k_norm,
              sinks, w_out, ffn_norm, w_up, conv_w, conv_b, w_down):
    B, S, _ = x.shape
    scale = HEAD_DIM ** -0.5
    for l in range(DEPTH):
        h = rmsnorm(x, attn_norm[l])
        z = h @ w_in[l]
        o1 = POOL_WIDTH
        o2 = o1 + Q_WIDTH
        o3 = o2 + KV_WIDTH
        o4 = o3 + KV_WIDTH
        u_pool = z[..., :o1]
        q = z[..., o1:o2].reshape(B, S, N_Q_HEADS, HEAD_DIM)
        k = z[..., o2:o3].reshape(B, S, N_KV_HEADS, HEAD_DIM)
        v = z[..., o3:o4].reshape(B, S, N_KV_HEADS, HEAD_DIM)
        gates = jax.nn.sigmoid((z[..., o4:] + b_gate[l]).astype(jnp.float32)).astype(x.dtype)
        g_pool, g_attn = gates[..., :D_MODEL], gates[..., D_MODEL:]

        a = pool_mixer(u_pool, w_pool[l], pool_scale[l])

        q = partial_rope(rmsnorm(q, q_norm[l]), positions) * scale
        k = partial_rope(rmsnorm(k, k_norm[l]), positions)
        b = swa_sink_attention(q, k, v, sinks[l])

        x = x + (g_pool * a + g_attn * b) @ w_out[l]

        h = rmsnorm(x, ffn_norm[l])
        up = causal_depthwise_conv(h @ w_up[l], conv_w[l], conv_b[l])
        gate, val = up[..., :D_FF], up[..., D_FF:]
        x = x + (jax.nn.silu(gate) * val) @ w_down[l]
    return x


N_META = 16
GRID_W = 64
DN_HEADS = 4
DN_HEAD_DIM = 128
DN_WIDTH = DN_HEADS * DN_HEAD_DIM
DN_CHUNK = 64
CONV_W = 5
AT_Q_HEADS = 8
AT_KV_HEADS = 2
AT_HEAD_DIM = 64
AT_WIDTH = AT_Q_HEADS * AT_HEAD_DIM
AT_KV_WIDTH = AT_KV_HEADS * AT_HEAD_DIM
Q_BLOCK = 128
ROPE_THETA_2 = 10000.0
ROPE_AXIS_DIM = AT_HEAD_DIM // 2
D_FF_2 = 4 * D_MODEL
MIX_WIDTH = DN_WIDTH + AT_WIDTH
IN_SIZES = (DN_WIDTH, DN_WIDTH, DN_WIDTH, DN_WIDTH, 2 * DN_HEADS, 2 * DN_HEADS, AT_WIDTH, AT_KV_WIDTH, AT_KV_WIDTH)
IN_COLS = 4 * DN_WIDTH + 4 * DN_HEADS + AT_WIDTH + 2 * AT_KV_WIDTH


def rms_norm(x, w):
    xf = x.astype(jnp.float32)
    y = xf * lax.rsqrt(jnp.mean(xf * xf, axis=-1, keepdims=True) + EPS)
    return (y * w.astype(jnp.float32)).astype(x.dtype)

def l2_norm(x):
    xf = x.astype(jnp.float32)
    return xf * lax.rsqrt(jnp.sum(xf * xf, axis=-1, keepdims=True) + EPS)

def short_conv_silu(x, w):
    C = x.shape[-1]
    y = lax.conv_general_dilated(
        x, w[:, None, :].astype(x.dtype), window_strides=(1,),
        padding=[(CONV_W // 2, CONV_W // 2)],
        dimension_numbers=('NWC', 'WIO', 'NWC'), feature_group_count=C)
    return jax.nn.silu(y)

def to_scan_order(a_fwd, a_bwd):
    pad = jnp.zeros((a_fwd.shape[0], DN_CHUNK - N_META) + a_fwd.shape[2:], a_fwd.dtype)
    fwd = jnp.concatenate([pad, a_fwd], axis=1)
    bwd = jnp.concatenate([pad, a_bwd[:, :N_META], jnp.flip(a_bwd[:, N_META:], axis=1)], axis=1)
    return jnp.concatenate([fwd, bwd], axis=0)

def chunk_gated_delta_rule(q, k, v, g, beta):
    N, T, H, K = q.shape
    V = v.shape[-1]
    C = DN_CHUNK
    n = T // C

    def chunks(a):
        return jnp.moveaxis(a.reshape((N, n, C, H) + a.shape[3:]), 3, 2)

    q, k, v, g, beta = chunks(q), chunks(k), chunks(v), chunks(g), chunks(beta)
    gc = jnp.cumsum(g, axis=-1)
    incl = jnp.tril(jnp.ones((C, C), dtype=bool))
    strict = jnp.tril(jnp.ones((C, C), dtype=bool), -1)
    decay = jnp.exp(jnp.where(incl, gc[..., :, None] - gc[..., None, :], -jnp.inf))
    kk = jnp.einsum('bnhik,bnhjk->bnhij', k, k)
    a_low = jnp.where(strict, kk * decay * beta[..., :, None], 0.0)
    rhs = jnp.concatenate([v * beta[..., None], k * (beta * jnp.exp(gc))[..., None]], axis=-1)
    uw = lax.linalg.triangular_solve(a_low + jnp.eye(C, dtype=a_low.dtype), rhs,
                                     left_side=True, lower=True, unit_diagonal=True)
    u, w = uw[..., :V], uw[..., V:]
    qk = jnp.einsum('bnhik,bnhjk->bnhij', q, k) * decay
    q_dec = q * jnp.exp(gc)[..., None]
    k_dec = k * jnp.exp(gc[..., -1:] - gc)[..., None]
    g_last = jnp.exp(gc[..., -1])

    def step(S, xs):
        q_i, k_i, u_i, w_i, qk_i, gl_i = xs
        v_new = u_i - jnp.einsum('bhck,bhkv->bhcv', w_i, S)
        o_i = jnp.einsum('bhck,bhkv->bhcv', q_i, S) + jnp.einsum('bhij,bhjv->bhiv', qk_i, v_new)
        S = S * gl_i[..., None, None] + jnp.einsum('bhck,bhcv->bhkv', k_i, v_new)
        return S, o_i

    xs = tuple(jnp.moveaxis(a, 1, 0) for a in (q_dec, k_dec, u, w, qk, g_last))
    S0 = jnp.zeros((N, H, K, V), jnp.float32)
    _, o = lax.scan(step, S0, xs)
    o = jnp.moveaxis(o, 0, 1)
    return jnp.moveaxis(o, 3, 2).reshape(N, T, H, V)

def gated_deltanet_group(q, k, v, z, b, a, conv_w, a_log, dt_bias, o_norm_w):
    B, L, _ = q.shape
    out_dtype = q.dtype
    qkv = short_conv_silu(jnp.concatenate([q, k, v], axis=-1), conv_w)
    q, k, v = jnp.split(qkv, 3, axis=-1)
    heads = lambda t: t.reshape(B, L, DN_HEADS, DN_HEAD_DIM)
    q = l2_norm(heads(q)) * (DN_HEAD_DIM ** -0.5)
    k = l2_norm(heads(k))
    v = heads(v).astype(jnp.float32)
    beta = jax.nn.sigmoid(b.astype(jnp.float32)).reshape(B, L, 2, DN_HEADS)
    g = -jnp.exp(a_log.astype(jnp.float32)) * jax.nn.softplus(
        a.astype(jnp.float32).reshape(B, L, 2, DN_HEADS) + dt_bias.astype(jnp.float32))
    o = chunk_gated_delta_rule(
        to_scan_order(q, q), to_scan_order(k, k), to_scan_order(v, v),
        to_scan_order(g[:, :, 0], g[:, :, 1]), to_scan_order(beta[:, :, 0], beta[:, :, 1]))
    pad = DN_CHUNK - N_META
    o_f = o[:B, pad:]
    o_b = o[B:, pad:]
    o_b = jnp.concatenate([o_b[:, :N_META], jnp.flip(o_b[:, N_META:], axis=1)], axis=1)
    o = o_f + o_b
    o = rms_norm(o, o_norm_w) * jax.nn.silu(heads(z).astype(jnp.float32))
    return o.reshape(B, L, DN_WIDTH).astype(out_dtype)

def axial_rope_angles(n_real):
    rows = n_real // GRID_W
    r, c = jnp.meshgrid(jnp.arange(rows), jnp.arange(GRID_W), indexing='ij')
    r = r.reshape(-1).astype(jnp.float32)
    c = c.reshape(-1).astype(jnp.float32)
    F = ROPE_AXIS_DIM // 2
    freqs = ROPE_THETA_2 ** (-jnp.arange(F, dtype=jnp.float32) / F)
    ang = jnp.concatenate([r[:, None] * freqs, c[:, None] * freqs], axis=-1)
    return jnp.concatenate([jnp.zeros((N_META, 2 * F), jnp.float32), ang], axis=0)

def apply_axial_rope(x, ang):
    B, L, H, D = x.shape
    F = ROPE_AXIS_DIM // 2
    xr = x.astype(jnp.float32).reshape(B, L, H, 2, 2, F)
    x1, x2 = xr[..., 0, :], xr[..., 1, :]
    an = ang.reshape(L, 1, 2, F)
    cos, sin = jnp.cos(an), jnp.sin(an)
    out = jnp.stack([x1 * cos - x2 * sin, x2 * cos + x1 * sin], axis=-2)
    return out.reshape(B, L, H, D).astype(x.dtype)

def axial_gqa_group(q, k, v, q_norm_w, k_norm_w):
    B, L, _ = q.shape
    G = AT_Q_HEADS // AT_KV_HEADS
    n_real = L - N_META
    q = rms_norm(q.reshape(B, L, AT_Q_HEADS, AT_HEAD_DIM), q_norm_w)
    k = rms_norm(k.reshape(B, L, AT_KV_HEADS, AT_HEAD_DIM), k_norm_w)
    v = v.reshape(B, L, AT_KV_HEADS, AT_HEAD_DIM)
    ang = axial_rope_angles(n_real)
    q = apply_axial_rope(q, ang) * (AT_HEAD_DIM ** -0.5)
    k = apply_axial_rope(k, ang)
    q = q.reshape(B, L, AT_KV_HEADS, G, AT_HEAD_DIM)

    def attend(qb):
        s = jnp.einsum('bqhgd,bkhd->bhgqk', qb, k, preferred_element_type=jnp.float32)
        p = jax.nn.softmax(s, axis=-1).astype(v.dtype)
        return jnp.einsum('bhgqk,bkhd->bqhgd', p, v)

    o_meta = attend(q[:, :N_META]).reshape(B, N_META, AT_WIDTH)
    nb = n_real // Q_BLOCK
    qr = q[:, N_META:].reshape(B, nb, Q_BLOCK, AT_KV_HEADS, G, AT_HEAD_DIM)
    o_real = lax.map(attend, jnp.moveaxis(qr, 1, 0))
    o_real = jnp.moveaxis(o_real, 0, 1).reshape(B, n_real, AT_WIDTH)
    return jnp.concatenate([o_meta, o_real], axis=1)

def second_inputs(seed: int = 0) -> dict:
    key = jax.random.key(seed)
    ks = jax.random.split(key, 20)
    f32 = jnp.float32
    nrm = lambda k_, shape, scale: jax.random.normal(k_, shape, f32) * scale
    gain = lambda k_, shape: 1.0 + 0.02 * jax.random.normal(k_, shape, f32)
    x = jax.random.normal(ks[0], (BATCH, SEQ, D_MODEL), f32)
    meta_tokens = nrm(ks[1], (N_META, D_MODEL), 1.0)
    w_in = nrm(ks[2], (DEPTH, D_MODEL, IN_COLS), D_MODEL ** -0.5)
    conv_w = nrm(ks[3], (DEPTH, CONV_W, 3 * DN_WIDTH), CONV_W ** -0.5)
    a_log = jnp.log(jax.random.uniform(ks[4], (DEPTH, 2, DN_HEADS), f32, 1.0, 16.0))
    dt = jnp.exp(jax.random.uniform(ks[5], (DEPTH, 2, DN_HEADS), f32, np.log(1e-3), np.log(1e-1)))
    dt_bias = dt + jnp.log(-jnp.expm1(-dt))
    dn_out_norm = gain(ks[6], (DEPTH, DN_HEAD_DIM))
    q_norm = gain(ks[7], (DEPTH, AT_HEAD_DIM))
    k_norm = gain(ks[8], (DEPTH, AT_HEAD_DIM))
    w_out = nrm(ks[9], (DEPTH, MIX_WIDTH, D_MODEL), MIX_WIDTH ** -0.5)
    norm_mix_pre = gain(ks[10], (DEPTH, D_MODEL))
    norm_mix_post = gain(ks[11], (DEPTH, D_MODEL))
    w_up = nrm(ks[12], (DEPTH, D_MODEL, D_FF_2), D_MODEL ** -0.5)
    w_down = nrm(ks[13], (DEPTH, D_FF_2, D_MODEL), D_FF_2 ** -0.5)
    norm_mlp_pre = gain(ks[14], (DEPTH, D_MODEL))
    norm_mlp_post = gain(ks[15], (DEPTH, D_MODEL))
    return {"x": x, "meta_tokens": meta_tokens, "w_in": w_in, "conv_w": conv_w,
            "a_log": a_log, "dt_bias": dt_bias, "dn_out_norm": dn_out_norm,
            "q_norm": q_norm, "k_norm": k_norm, "w_out": w_out,
            "norm_mix_pre": norm_mix_pre, "norm_mix_post": norm_mix_post,
            "w_up": w_up, "w_down": w_down,
            "norm_mlp_pre": norm_mlp_pre, "norm_mlp_post": norm_mlp_post}

def second_block(x, meta_tokens, w_in, conv_w, a_log, dt_bias, dn_out_norm, q_norm, k_norm, w_out,
              norm_mix_pre, norm_mix_post, w_up, w_down, norm_mlp_pre, norm_mlp_post):
    B = x.shape[0]
    split_points = [int(s) for s in np.cumsum(IN_SIZES)[:-1]]
    meta = jnp.broadcast_to(meta_tokens[None].astype(x.dtype), (B, N_META, D_MODEL))
    h = jnp.concatenate([meta, x], axis=1)
    for l in range(DEPTH):
        u = rms_norm(h, norm_mix_pre[l])
        proj = u @ w_in[l]
        dq, dk, dv, dz, db, da, aq, ak, av = jnp.split(proj, split_points, axis=-1)
        o_dn = gated_deltanet_group(dq, dk, dv, dz, db, da, conv_w[l], a_log[l], dt_bias[l], dn_out_norm[l])
        o_at = axial_gqa_group(aq, ak, av, q_norm[l], k_norm[l])
        mix = jnp.concatenate([o_dn, o_at.astype(o_dn.dtype)], axis=-1) @ w_out[l]
        h = h + rms_norm(mix, norm_mix_post[l])
        u = rms_norm(h, norm_mlp_pre[l])
        f = jnp.square(jax.nn.relu(u @ w_up[l])) @ w_down[l]
        h = h + rms_norm(f, norm_mlp_post[l])
    return h[:, N_META:]


def setup_inputs(seed=0):
    out = dict(first_inputs(seed))
    for name, value in second_inputs(seed + 1).items():
        if name != "x":
            out[name + "_2"] = value
    return out


def reference(
    x, positions, attn_norm, w_in, b_gate, w_pool, pool_scale, q_norm, k_norm, sinks, w_out,
    ffn_norm, w_up, conv_w, conv_b, w_down, meta_tokens_2, w_in_2, conv_w_2, a_log_2, dt_bias_2,
    dn_out_norm_2, q_norm_2, k_norm_2, w_out_2, norm_mix_pre_2, norm_mix_post_2, w_up_2,
    w_down_2, norm_mlp_pre_2, norm_mlp_post_2,
):
    x = first_block(
        x, positions, attn_norm, w_in, b_gate, w_pool, pool_scale, q_norm, k_norm, sinks, w_out,
        ffn_norm, w_up, conv_w, conv_b, w_down,
    )
    return second_block(
        x, meta_tokens_2, w_in_2, conv_w_2, a_log_2, dt_bias_2, dn_out_norm_2, q_norm_2,
        k_norm_2, w_out_2, norm_mix_pre_2, norm_mix_post_2, w_up_2, w_down_2, norm_mlp_pre_2,
        norm_mlp_post_2,
    )


_drawn_inputs = setup_inputs


def setup_inputs(seed=0):
    import zlib

    import numpy as np

    out = dict(_drawn_inputs(seed))
    spreads = {}
    factors = {'q_norm': 8.0,
     'k_norm': 8.0,
     'sinks': 53.69,
     'conv_b': 3.098,
     'dn_out_norm_2': 11.736,
     'q_norm_2': 24.29,
     'k_norm_2': 24.654,
     'norm_mix_pre_2': 2.869,
     'norm_mix_post_2': 4.116,
     'norm_mlp_pre_2': 15.132,
     'norm_mlp_post_2': 57.929}
    for name, (base, spread) in spreads.items():
        noise = np.random.default_rng([zlib.crc32(name.encode()), seed]).standard_normal(out[name].shape)
        drawn = base * np.exp(spread * noise) if base else spread * noise
        out[name] = __import__('jax').numpy.asarray(drawn.astype(out[name].dtype))
    for name, factor in factors.items():
        out[name] = (out[name] * factor).astype(out[name].dtype)
    return out
```

```python
from contextlib import ExitStack

import concourse.bass as bass
import numpy as np
from concourse import mybir

P = 128
F32 = mybir.dt.float32
F32R = mybir.dt.float32r
I32 = mybir.dt.int32
ALU = mybir.AluOpType
ACT = mybir.ActivationFunctionType
AX = mybir.AxisListType.X

T = 512
META = 16
L = META + T
HALF = L // 2
D = 1024
KT = D // P
EPS = 1e-6
FF = 2816
FT = FF // P
FF2 = 4 * D
FT2 = FF2 // P
NB = T // P
NLEV = 6

U_POOLIN = 0
U_KV = U_POOLIN + 8
U_Q = U_KV + 2
U_PM = U_Q + 8
U_GATE = U_PM + 2
U_OUT = U_GATE + 16
U_UP = U_OUT + 8
U_DOWN = U_UP + 2 * FT
U_AT2 = U_DOWN + FT
U_DN2 = U_AT2 + 6
U_OUT2 = U_DN2 + 16
U_UP2 = U_OUT2 + 8
U_DOWN2 = U_UP2 + FT2
N_UNITS = U_DOWN2 + FT2
assert N_UNITS % 4 == 0 and U_OUT2 % 4 == 0

_V = [("attn_norm", 8), ("b_gate", 16), ("pool_scale", 8), ("q_norm", 1), ("k_norm", 1), ("sinks", 16),
      ("ffn_norm", 8), ("conv_w", 3 * 2 * FT), ("conv_b", 2 * FT), ("mix_pre", 8), ("mix_post", 8),
      ("mlp_pre", 8), ("mlp_post", 8), ("dconv", 5 * 12), ("a_log", 8), ("dt_bias", 8), ("dn_norm", 1),
      ("q_norm2", 1), ("k_norm2", 1)]
VOFF = {}
NV = 0
for _n, _w in _V:
    VOFF[_n] = NV
    NV += _w

_C = [("ident", P), ("blk64", P), ("rot2", P), ("swap", P), ("upto_f", P), ("upto_b", P),
      ("lev_f", (NLEV + 1) * P), ("lev_b", (NLEV + 1) * P), ("half_pi", 1), ("eps", 1), ("eps4", 1), ("eps512", 1)]
COFF = {}
NCST = 0
for _n, _w in _C:
    COFF[_n] = NCST
    NCST += _w
NC1 = P + 256 + 64 + 1
NC2 = 2 * L


def constants():
    eye = np.eye(P, dtype=np.float32)
    i = np.arange(P)
    c = np.zeros((P, NCST), np.float32)

    def put(name, a):
        c[:, COFF[name]:COFF[name] + a.shape[1]] = a

    put("ident", eye)
    put("blk64", (i[:, None] // 64 == i[None, :] // 64).astype(np.float32))
    put("swap", (i[:, None] == (i[None, :] + 64) % P).astype(np.float32))
    rot2 = np.zeros((P, P), np.float32)
    for m in range(P):
        if m % 32 < 16:
            rot2[m + 16, m] = -1.0
        else:
            rot2[m - 16, m] = 1.0
    put("rot2", rot2)
    put("upto_f", (i[:, None] <= i[None, :]).astype(np.float32))
    put("upto_b", (i[:, None] >= i[None, :]).astype(np.float32))
    lev = []
    for n in range(NLEV + 1):
        b = 1 << n
        row, col = i[:, None] // b, i[None, :] // b
        lev.append(((row % 2 == 1) & (col == row - 1)).astype(np.float32))
    put("lev_f", np.concatenate([m.T for m in lev], 1))
    put("lev_b", np.concatenate(lev, 1))
    put("half_pi", np.full((P, 1), np.pi / 2, np.float32))
    put("eps", np.full((P, 1), EPS, np.float32))
    put("eps4", np.full((P, 1), 4 * EPS, np.float32))
    put("eps512", np.full((P, 1), 512 * EPS, np.float32))
    c1 = np.zeros((P, NC1), np.float32)
    for m in range(P):
        if m % 64 < 8:
            c1[m + 8, m] = -1.0
        elif m % 64 < 16:
            c1[m - 8, m] = 1.0
    k = np.arange(256)
    ok = (k[None, :] <= i[:, None] + P) & (i[:, None] + P - k[None, :] < P)
    c1[:, P:P + 256] = np.where(ok, 0.0, -1e30)
    for g, w in enumerate((2, 4, 8, 16)):
        c1[:, P + 256 + 16 * g:P + 272 + 16 * g] = np.minimum(np.arange(16) + 1, w)
    inv = np.float32(500000.0) ** (-np.arange(0, 16, 2, dtype=np.float32) / np.float32(16))
    c1[:, NC1 - 1] = np.where(i % 64 < 16, inv[i % 8], 0.0)
    t = np.arange(T)
    freqs = np.float32(10000.0) ** (-np.arange(16, dtype=np.float32) / np.float32(16))
    ang = np.zeros((P, L), np.float32)
    for m in range(P):
        x = (t // 64 if m % 64 < 32 else t % 64).astype(np.float32)
        ang[m, META:] = x * freqs[m % 16]
    return c, c1, np.concatenate([np.cos(ang), np.sin(ang)], 1).astype(np.float32)


def wait(eng, sem, value):
    if isinstance(value, int) and value <= 0:
        return
    eng.wait_ge(sem, value)


PE_M = ["A", "T", "P1", "XY1", "P2", "XY2", "P3", "XY3", "KV", "VN", "OS"]
DVE_M = ["D", "E", "X", "XY1", "XY2", "XY3", "KV", "O"]
ACT_M = ["E", "P1", "P2", "P3", "VN"]
PE_R = ["A", "T"] + [f"{s}{n}" for n in range(1, 7) for s in ("P", "XY")] + ["KV", "KS", "VN", "OS"]
DVE_R = ["D", "E", "X"] + [f"XY{n}" for n in range(1, 7)] + ["KV", "R", "O"]
ACT_R = ["E"] + [f"P{n}" for n in range(1, 7)] + ["VN"]


def _stage(meta, real):
    def at(st, name):
        return meta.index(name) + 1 if st < 0 else len(meta) + st * len(real) + real.index(name) + 1
    return at


pe_at, dve_at, act_at = _stage(PE_M, PE_R), _stage(DVE_M, DVE_R), _stage(ACT_M, ACT_R)


class Steps:

    def __init__(self, eng, sem, base=0):
        self.eng, self.sem, self.base, self.n = eng, sem, base, 0

    def __call__(self, ins):
        ins.then_inc(self.sem, 1)
        self.n += 1

    def settle(self):
        self.eng.wait_ge(self.sem, self.base + self.n)


def build(nc, w_stream, w_ba, x_t, vec, cst, cst1, cst2, pos, out):
    ctx = ExitStack()
    with ctx:
        def sb(name, shape, dt=F32):
            return ctx.enter_context(nc.sbuf_tensor(name, shape, dt))

        def sem(name):
            return ctx.enter_context(nc.semaphore(name))

        ps = ctx.enter_context(nc.psum_tensor("ps", [P, 8, 512], F32))
        raw = [sb(f"raw{i}", [P, 8, P]) for i in range(2)]
        w_hi = [sb(f"w_hi{i}", [P, 8, P], F32R) for i in range(4)]
        w_lo = [sb(f"w_lo{i}", [P, 8, P], F32R) for i in range(4)]
        xT = sb("xT", [P, KT, L])
        h_hi = sb("h_hi", [P, KT, L], F32R)
        h_lo = sb("h_lo", [P, KT, L], F32R)
        g_hi = sb("g_hi", [P, 4, T], F32R)
        g_lo = sb("g_lo", [P, 4, T], F32R)
        C = sb("C", [P, NCST])
        V = sb("V", [P, NV])
        ones = sb("ones", [P, P])
        AC = 22080
        arena = sb("arena", [P, AC])

        def cst_ap(name, w=P, at=0):
            return C[:, COFF[name] + at:COFF[name] + at + w]

        def vcol(name, i=0):
            return V[:, VOFF[name] + i:VOFF[name] + i + 1]

        class Area:

            def __init__(self, at=0):
                self.at = at

            def __call__(self, *shape):
                n = int(np.prod(shape))
                a = arena[:, self.at:self.at + n]
                self.at += n
                assert self.at <= AC, (self.at, AC)
                if len(shape) == 2:
                    a = a.rearrange("p (a b) -> p a b", b=shape[1])
                if len(shape) == 3:
                    a = a.rearrange("p (a b c) -> p a b c", b=shape[1], c=shape[2])
                return a

        ar = Area()
        U = ar(8, L)
        Q = ar(8, T)
        KA, KB = ar(T), ar(T)
        vtok = ar(NB, P)
        small = ar(64)
        mid = ar.at
        rope_c, rope_s = ar(T), ar(T)
        rot1 = ar(P)
        W0, W1 = ar(2, L), ar(2, L)
        vT = ar(T)
        sqb, qgb = ar(2, T), ar(2, T)
        rs, rinv, t1, t2 = ar(2, T), ar(T), ar(T), ar(T)
        ang, nrd, ab = t1, t2, rinv
        posi = rs[:, 0, :].bitcast(I32)
        posf = rs[:, 1, :]
        GA = arena[:, mid:mid + 8 * T].rearrange("p (a b) -> p a b", b=T)
        ar.at = mid + 8 * T
        sm = [ar(4, 256), ar(4, 256)]
        pT = ar(2, 512)
        tg = ar(2, T)
        band = sb("band", [P, 256 + 64 + 1])
        cnt16 = band[:, 256:320]
        invf = band[:, 320:321]
        nrm = Area(AC - 4 * L)
        n_sq = nrm(2, L)
        n_h = nrm(2, L)
        n_rs = arena[:, AC - 5 * L:AC - 4 * L]
        n_ri = arena[:, AC - 6 * L:AC - 5 * L]
        ar = Area()
        M1 = ar(FT, T)
        cg, cv, eg = ar(2, T), ar(2, T), ar(2, T)
        ar = Area()
        DQ, DK, DV = ar(4, L), ar(4, L), ar(4, L)
        DZ = ar(4, T)
        AQ = ar(4, T)
        OD = ar(4, T)
        G, BETA, BH, NBE, KD, EGL, GCC = (ar(5, 8) for _ in range(7))
        tb = [ar(5, 8) for _ in range(4)]
        small2 = ar(16)
        p4 = ar.at
        AKA, AKB = ar(L), ar(L)
        avtok = ar(5, P)
        c2, s2 = ar(L), ar(L)
        x5 = ar(2, L + 4)
        y5, e5, r5, i5 = ar(L), ar(L), ar(L), ar(L)
        s5 = OD[:, 0:2, :].rearrange("p a b -> p (a b)")[:, 0:L]
        pp = [ar(640), ar(640)]
        ppT = OD[:, 2:4, :].rearrange("p a b -> p (a b)")[:, 0:640].rearrange("p (a b) -> p a b", b=P)
        ar.at = p4
        lane = [{n: ar(4, P) for n in ("EM", "QE", "QD", "AT", "X", "Y", "P")} for _ in range(2)]
        ST = [ar(4, P) for _ in range(2)]
        ar = Area()
        M2 = ar(FT2, T)
        rb = ar(4, T)
        F2 = arena[:, 0:8 * T].rearrange("p (a b) -> p a b", b=T)
        wba32 = n_sq.rearrange("p a b -> p (a b)")[:, 0:KT * 16].rearrange("p (a b) -> p a b", b=16)
        wba_hi = sb("wba_hi", [P, KT, 16], F32R)
        wba_lo = sb("wba_lo", [P, KT, 16], F32R)

        raw_ready = [sem(f"raw_ready{i}") for i in range(2)]
        split_done = [sem(f"split_done{i}") for i in range(4)]
        unit_done = [sem(f"unit_done{i}") for i in range(4)]
        names = ("pool_step act_step dve_step act_up dve_up tile_read qk_side qk_sqrt qk_dve kb_done kb_ready v_turned v_ready "
                 "rope_ready pads_ready win_ready pg_ready pm_read sq_ready sq_used rs_ready hn_ready hi_ready h_ready x_ready "
                 "s_ready s_read mx_ready exp_ready p_ready pT_ready pT_copied pv_done o_read gp_done "
                 "up_act up_read m1_ready silu_ready relu_ready ms_hi ms_ready m2_ready f2_ready "
                 "ba_split ba_done t2_read k2_act k2_side k2_sqrt k2_dve kb2_done kb2_ready v2_turned v2_ready "
                 "dn_act dn_dve dn_c c_act dn_sq dn_ss dn_sqrt dn_ready "
                 "s2_ready mx2_ready e2_ready p2_ready pT2_ready pT2_copied o2_done o2_read "
                 "ba_ready gc_done tab_ready on_sq on_ss on_rs mix_read "
                 "v_loaded c_loaded x_loaded misc_loaded c2_loaded ba_loaded ones_ready out_done fold_ready").split()
        S = {n: sem(n) for n in names}
        dn_pe = [sem(f"dn_pe{i}") for i in range(2)]
        dn_v = [sem(f"dn_v{i}") for i in range(2)]
        dn_a = [sem(f"dn_a{i}") for i in range(2)]
        dn_p = [sem(f"dn_p{i}") for i in range(2)]

        def rounds(u, i=0):
            return u // 4 + i + 1

        def product(eng, u, i=0):
            eng.wait_ge(unit_done[u % 4], rounds(u, i))

        def rep(eng, n, body, first=1):
            for i in range(min(first, n)):
                body(i)
            if n > first:
                with eng.Fori(first, n, 1) as i:
                    body(i)

        def ds(i, n=1):
            return slice(i, i + n) if isinstance(i, int) else bass.ds(i, n)

        REAL = slice(META, L)
        halves = [slice(0, HALF), slice(HALF, L)]

        block = ctx.enter_context(nc.Block())

        @block.sync
        def _(sp):
            for k in range(0, KT, 4):
                sp.dma_start(xT[:, k:k + 4, :], x_t[:, k:k + 4, :]).then_inc(S["x_loaded"], 16)
            sp.dma_start(V[:], vec).then_inc(S["v_loaded"], 16)

            def load(i):
                for j in range(4):
                    if j >= 2:
                        sp.wait_ge(split_done[j - 2], i + 1)
                    elif not isinstance(i, int) or i > 0:
                        sp.wait_ge(split_done[j + 2], i)
                    sp.dma_start(raw[j % 2][:].rearrange("p a b -> p (a b)"),
                                 w_stream[ds(4 * i + j), :, :].rearrange("a p n -> p (a n)")
                                 ).then_inc(raw_ready[j % 2], 16)
                if isinstance(i, int) and i == 0:
                    sp.dma_start(C[:], cst).then_inc(S["c_loaded"], 16)
                    sp.dma_start(rot1, cst1[:, 0:P]).then_inc(S["misc_loaded"], 16)
                    sp.dma_start(band[:], cst1[:, P:]).then_inc(S["misc_loaded"], 16)
                    sp.dma_start(posi, pos).then_inc(S["misc_loaded"], 16)

            N_FIRST = -(-U_AT2 // 4)
            rep(sp, N_FIRST, load)
            sp.wait_ge(S["h_ready"], 32)
            sp.dma_start(arena[:, p4 + 2 * L + 640:p4 + 4 * L + 640], cst2).then_inc(S["c2_loaded"], 16)
            sp.dma_start(wba32, w_ba).then_inc(S["ba_loaded"], 16)
            with sp.Fori(N_FIRST, N_UNITS // 4, 1) as i:
                load(i)
            for f in range(KT):
                sp.wait_ge(S["x_ready"], 24 + f + 1)
                sp.dma_start(out[:, f, :], xT[:, f, REAL]).then_inc(S["out_done"], 16)
            sp.wait_ge(S["out_done"], 16 * KT)

        @block.gpsimd
        def _(pool):
            def split(i):
                for j in range(4):
                    pool.wait_ge(raw_ready[j % 2], 16 * (2 * i + j // 2 + 1))
                    if not isinstance(i, int) or i > 0:
                        pool.wait_ge(unit_done[j], i)
                    pool.nop(nofuse=True)
                    pool.wait_ge(S["ones_ready"], 1)
                    pool.tensor_scalar(w_hi[j][:], raw[j % 2][:], 1.0, 1.0, ALU.mult, ALU.mult).then_inc(S["pool_step"], 1)
                    pool.wait_ge(S["pool_step"], 4 * i + j + 1)
                    pool.tensor_tensor(w_lo[j][:], raw[j % 2][:], w_hi[j][:], ALU.subtract).then_inc(split_done[j], 1)

            n = U_OUT2 // 4 + 1
            rep(pool, n, split)
            for st in range(NB):
                for lev in range(1, NLEV + 1):
                    for d in range(2):
                        b = lane[d]
                        m = cst_ap("lev_b" if d else "lev_f", P, P * lev)
                        pool.wait_ge(dn_v[d], dve_at(st, "E"))
                        if lev > 1:
                            pool.wait_ge(dn_pe[d], pe_at(st, f"P{lev - 1}"))
                        pool.tensor_tensor(b["EM"], b["AT"], m.unsqueeze(1).to_broadcast([P, 4, P]), ALU.mult).then_inc(dn_p[d], 1)
            with pool.Fori(n, N_UNITS // 4, 1) as i:
                split(i)

        @block.scalar
        def _(act):
            step = Steps(act, S["act_step"])

            def a(o, i, f, **kw):
                return nc.scalar.activation(o, i, f, **kw)

            def square(n, f, src, cols):
                wait(act, S["sq_used"], 8 * n + f - 1)
                a(n_sq[:, f % 2, 0:cols], src, ACT.Square).then_inc(S["sq_ready"], 1)

            def root(n, src, dst):
                act.wait_ge(S["sq_used"], 8 * (n + 1))
                a(dst, src, ACT.Sqrt, scale=1.0 / D, bias=cst_ap("eps", 1)).then_inc(S["rs_ready"], 1)

            def high(n, cols):
                for f in range(KT):
                    act.wait_ge(S["hn_ready"], 8 * n + f + 1)
                    a(h_hi[:, f, cols], n_h[:, f % 2, 0:cols.stop - cols.start], ACT.Copy).then_inc(S["hi_ready"], 1)

            act.wait_ge(S["c_loaded"], 16)
            act.wait_ge(S["x_loaded"], 32)
            for f in range(KT):
                square(0, f, xT[:, f, REAL], T)
            root(0, ps[:, 7, :], n_rs[:, 0:T])
            high(0, REAL)
            act.wait_ge(S["rope_ready"], 2)
            a(rope_s, nrd, ACT.Sin).then_inc(S["rope_ready"], 1)
            a(rope_c, ab, ACT.Sin, scale=-1.0, bias=cst_ap("half_pi", 1)).then_inc(S["rope_ready"], 1)
            for f in range(8):
                product(act, U_POOLIN + f)
                a(U[:, f, REAL], ps[:, f % 2, :], ACT.Copy).then_inc(S["tile_read"], 1)

            def qk_in(t, n, u, gain):
                product(act, u)
                wait(act, S["qk_side"], t - 1)
                wait(act, S["qk_dve"], t - 1)
                if t == 0:
                    act.wait_ge(S["rope_ready"], 4)
                a(sqb[:, t % 2, :], ps[:, n % 2, :], ACT.Square)
                a(qgb[:, t % 2, :], ps[:, n % 2, :], ACT.Copy, scale=gain).then_inc(S["tile_read"], 1)

            def qk_root(t):
                act.wait_ge(S["qk_side"], t + 1)
                a(rs[:, t % 2, :], ps[:, 2 + t % 2, :], ACT.Sqrt, scale=1.0 / 64, bias=cst_ap("eps", 1)).then_inc(S["qk_sqrt"], 1)

            qk_in(0, 8, U_KV, vcol("k_norm"))
            product(act, U_KV + 1)
            a(vT, ps[:, 1, :], ACT.Copy).then_inc(S["tile_read"], 1)
            qk_root(0)
            for t in range(1, 9):
                qk_in(t, 9 + t, U_Q + t - 1, vcol("q_norm"))
                if t == 1:
                    act.wait_ge(S["kb_done"], 1)
                    a(KB, ps[:, 6, :], ACT.Copy).then_inc(S["kb_ready"], 1)
                    act.wait_ge(S["v_turned"], 1)
                    a(vtok.rearrange("p a b -> p (a b)"), ps[:, 7, :], ACT.Copy).then_inc(S["v_ready"], 1)
                if t > 1:
                    qk_root(t - 1)
            qk_root(8)

            def pooled_out(k):
                product(act, U_PM + k)
                for j in range(4):
                    a(U[:, 4 * k + j, REAL], ps[:, 2 + j, :], ACT.Copy, scale=vcol("pool_scale", 4 * k + j)).then_inc(S["pm_read"], 1)

            def gate(i):
                product(act, U_GATE + i)
                if i == 0:
                    act.wait_ge(S["qk_dve"], 9)
                    act.wait_ge(S["v_turned"], 1)
                    act.wait_ge(S["win_ready"], 4)
                if i < 8:
                    a(GA[:, i, :], ps[:, i % 2, :], ACT.Tanh, scale=0.5, bias=vcol("b_gate", 8 + i)).then_inc(S["tile_read"], 1)
                else:
                    wait(act, S["gp_done"], i - 9)
                    a(tg[:, i % 2, :], ps[:, i % 2, :], ACT.Tanh, scale=0.5, bias=vcol("b_gate", i - 8)).then_inc(S["tile_read"], 1)

            pooled_out(0)
            gate(0)
            gate(1)
            pooled_out(1)

            def exps(n):
                s = sm[n % 2] if n >= 4 else sm[n % 2][:, :, P:2 * P]
                act.wait_ge(S["mx_ready"], n + 1)
                b = 16 * (n % 2)
                for m in range(4):
                    a(s[:, m, :], s[:, m, :], ACT.Exp, bias=small[:, b + m:b + m + 1], accum_out=small[:, b + 8 + m:b + 9 + m])
                a(small[:, b + 12:b + 16], small[:, b + 4:b + 8], ACT.Exp).then_inc(S["exp_ready"], 1)

            def turned(n):
                act.wait_ge(S["pT_ready"], n + 1)
                wait(act, S["pv_done"], n)
                if n >= 4:
                    a(pT[:, 0, :], ps[:, 4, :], ACT.Copy)
                a(pT[:, 1, :], ps[:, 5, :], ACT.Copy).then_inc(S["pT_copied"], 1)

            exps(0)
            exps(1)
            for n in range(16):
                turned(n)
                if n < 14:
                    exps(n + 2)
                    gate(n + 2)
            high(1, REAL)
            for f in range(KT):
                act.wait_ge(S["x_ready"], f + 1)
                square(1, f, xT[:, f, REAL], T)
            root(1, ps[:, 7, :], n_rs[:, 0:T])
            high(2, REAL)

            def up(i):
                for h in range(2):
                    j = 2 * i + h
                    for e, dst in ((0, cg), (1, cv)):
                        q = 2 * h + e
                        product(act, U_UP + q, i)
                        if isinstance(i, int):
                            wait(act, S["m1_ready"], j - 1)
                        else:
                            act.wait_ge(S["m1_ready"], 2 * i + (h - 1))
                        a(dst[:, h, :], ps[:, q, :], ACT.Identity, scale=V[:, ds(j + VOFF["conv_w"] + 2 * 2 * FT + e * FT)],
                          bias=V[:, ds(j + VOFF["conv_b"] + e * FT)]).then_inc(S["up_act"], 1)
                    act.wait_ge(S["up_read"], 4 * i + 2 * h + 1)
                    a(eg[:, h, :], cg[:, h, :], ACT.Silu).then_inc(S["silu_ready"], 1)

            rep(act, FT // 2, up)

            def m_high(src, n0, cnt):
                def body(i):
                    for j in range(4):
                        k = 4 * i + j
                        if isinstance(i, int):
                            wait(act, unit_done[(us + j) % 4], ring_before(us, j, i))
                        else:
                            act.wait_ge(unit_done[(us + j) % 4], ring_before(us, j, i))
                        a(g_hi[:, j, :], src[:, ds(k), :].rearrange("p a b -> p (a b)"), ACT.Copy).then_inc(S["ms_hi"], 1)
                return body

            def ring_before(us, j, i):
                return (us + j) // 4 + i

            us = U_DOWN
            act.wait_ge(S["m1_ready"], FT)
            rep(act, 5, m_high(M1, 0, FT))
            m_tail = m_high(M1, 0, FT)
            for j in range(2):
                act.wait_ge(unit_done[(us + j) % 4], ring_before(us, j, 5))
                a(g_hi[:, j, :], M1[:, 20 + j, :], ACT.Copy).then_inc(S["ms_hi"], 1)
            for f in range(KT):
                act.wait_ge(S["x_ready"], 8 + f + 1)
                square(2, f, xT[:, f, :], L)
            root(2, ps[:, 0:2, 0:HALF], n_rs.rearrange("p (a b) -> p a b", a=2))
            high(3, slice(0, L))

            act.wait_ge(S["ba_loaded"], 16)
            a(wba_hi[:], wba32, ACT.Copy).then_inc(S["ba_split"], 1)

            def two(t, n=0):
                return ps[:, 2 * (t % 2):2 * (t % 2) + 2, 0:HALF]

            def flat(x):
                return x.rearrange("p (a b) -> p a b", a=2)

            def k2_in(t, n, u, gain):
                product(act, u)
                wait(act, S["k2_side"], t)
                wait(act, S["k2_dve"], t)
                a(flat(s5), two(n), ACT.Square)
                a(flat(e5), two(n), ACT.Copy, scale=gain).then_inc(S["t2_read"], 1)

            def k2_root(t):
                act.wait_ge(S["k2_side"], t + 1)
                a(flat(r5), ps[:, 4:6, 0:HALF], ACT.Sqrt, scale=1.0 / 64, bias=cst_ap("eps", 1)).then_inc(S["k2_sqrt"], 1)

            k2_in(0, 0, U_AT2, vcol("k_norm2"))
            product(act, U_AT2 + 1)
            a(flat(x5[:, 1, 0:L]), two(1), ACT.Copy).then_inc(S["t2_read"], 1)
            k2_root(0)
            act.wait_ge(S["kb2_done"], 1)
            a(flat(AKB), ps[:, 4:6, 0:HALF], ACT.Copy).then_inc(S["kb2_ready"], 1)
            act.wait_ge(S["v2_turned"], 1)
            a(avtok[:, 0:4, :].rearrange("p a b -> p (a b)"), ps[:, 6, :], ACT.Copy)
            a(avtok[:, 4, :], ps[:, 7, 0:P], ACT.Copy).then_inc(S["v2_ready"], 1)
            for t in range(1, 5):
                k2_in(t, 1 + t, U_AT2 + 1 + t, vcol("q_norm2"))
                k2_root(t)

            act.wait_ge(S["ba_done"], 1)
            act.wait_ge(S["ba_ready"], 1)
            a(tb[0], ps[:, 7, 0:80].rearrange("p (a b) -> p a b", b=16)[:, :, 0:8], ACT.Tanh, scale=0.5)
            a(tb[2], tb[2], ACT.Exp, scale=-1.0)
            a(small2[:, 8:16], V[:, VOFF["a_log"]:VOFF["a_log"] + 8], ACT.Exp).then_inc(S["tab_ready"], 1)
            act.wait_ge(S["ba_ready"], 2)
            a(NBE, tb[3], ACT.Ln).then_inc(S["tab_ready"], 1)
            gc = ps[:, 6, 0:40].rearrange("p (a b) -> p a b", b=8)
            gl = ps[:, 6, 40:80].rearrange("p (a b) -> p a b", b=8)
            act.wait_ge(S["gc_done"], 1)
            act.wait_ge(S["ba_ready"], 4)
            a(EGL, gl, ACT.Exp)
            a(tb[1], gc, ACT.Exp)
            a(KD, KD, ACT.Exp).then_inc(S["tab_ready"], 1)

            def exp2(n):
                act.wait_ge(S["mx2_ready"], n + 1)
                a(flat(pp[n % 2][:, 0:L]), ps[:, 4:6, 0:HALF], ACT.Exp, bias=small2[:, n % 2:n % 2 + 1],
                  accum_out=small2[:, 2 + n % 2:3 + n % 2]).then_inc(S["e2_ready"], 1)

            def turned2(n):
                act.wait_ge(S["pT2_ready"], n + 1)
                wait(act, S["o2_done"], n)
                a(ppT[:, 0:4, :].rearrange("p a b -> p (a b)"), ps[:, 6, :], ACT.Copy)
                a(ppT[:, 4, :], ps[:, 7, 0:P], ACT.Copy).then_inc(S["pT2_copied"], 1)

            def dn_copy(d):
                product(act, U_DN2 + d)
                wait(act, S["dn_c"], d - 1)
                a(flat(x5[:, d % 2, 2:L + 2]), two(d), ACT.Copy).then_inc(S["t2_read"], 1)
                if d < 12:
                    wait(act, S["dn_c"], d)
                    act.wait_ge(S["t2_read"], 6 + d + 1)
                    a(y5, x5[:, d % 2, 2:L + 2], ACT.Copy, scale=vcol("dconv", 24 + d)).then_inc(S["c_act"], 1)

            def dn_tanh(d):
                wait(act, S["dn_c"], d)
                if d < 12:
                    act.wait_ge(S["dn_dve"], d + 1)
                    a(e5, y5, ACT.Tanh, scale=0.5).then_inc(S["c_act"], 1)
                else:
                    act.wait_ge(S["t2_read"], 6 + d + 1)
                    a(e5[:, 0:T], x5[:, d % 2, 2 + META:2 + L], ACT.Tanh, scale=0.5).then_inc(S["c_act"], 1)

            def dn_square(d):
                act.wait_ge(S["dn_c"], d + 1)
                a(s5, (DQ if d < 4 else DK)[:, d % 4, :], ACT.Square).then_inc(S["dn_sq"], 1)

            def dn_root(d):
                act.wait_ge(S["dn_ss"], d + 1)
                wait(act, S["dn_ready"], d)
                q = d < 4
                a(flat(r5), two(d), ACT.Sqrt, scale=float(P) if q else 1.0, bias=cst_ap("eps512" if q else "eps4", 1)
                  ).then_inc(S["dn_sqrt"], 1)

            exp2(0)
            exp2(1)
            for n in range(32):
                d = n // 2
                turned2(n)
                if n < 30:
                    exp2(n + 2)
                if n % 2 == 0:
                    if 1 <= d <= 8:
                        dn_root(d - 1)
                    dn_copy(d)
                else:
                    dn_tanh(d)
                    if d < 8:
                        dn_square(d)

            for st in range(-1, NB):
                for i, name in enumerate(ACT_M if st < 0 else ACT_R):
                    for d in range(2):
                        b, L0, L2 = lane[d], 4 * d, 4 * d + 2
                        r = slice(0, META if st < 0 else P)
                        w = META if st < 0 else P
                        if name == "E":
                            act.wait_ge(dn_v[d], dve_at(st, "D"))
                            if st >= 0:
                                a(b["QE"], ps[:, L0, :].rearrange("p (a b) -> p a b", b=P), ACT.Exp)
                            a(b["EM"][r, :, 0:w], b["EM"][r, :, 0:w], ACT.Exp).then_inc(dn_a[d], 1)
                        elif name[0] == "P":
                            act.wait_ge(dn_pe[d], pe_at(st, name))
                            a(b["P"][r, :, 0:w], ps[r, L0, 0:4 * w].rearrange("p (a b) -> p a b", b=w), ACT.Copy).then_inc(dn_a[d], 1)
                        elif name == "VN":
                            act.wait_ge(dn_pe[d], pe_at(st, name))
                            a(b["EM"][r, :, :], ps[r, L2, :].rearrange("p (a b) -> p a b", b=P), ACT.Copy).then_inc(dn_a[d], 1)

            for h in range(4):
                act.wait_ge(dn_v[0], dve_at(NB - 1, "O"))
                act.wait_ge(dn_v[1], dve_at(NB - 1, "O"))
                wait(act, S["on_ss"], h - 1)
                a(n_sq[:, h % 2, 0:T], OD[:, h, :], ACT.Square).then_inc(S["on_sq"], 1)
                act.wait_ge(S["on_ss"], h + 1)
                wait(act, S["hn_ready"], 32 + h)
                a(n_rs[:, 0:T], ps[:, h % 2, :], ACT.Sqrt, scale=1.0 / P, bias=cst_ap("eps", 1)).then_inc(S["on_rs"], 1)
                act.wait_ge(S["hn_ready"], 32 + h + 1)
                a(h_hi[:, h, REAL], n_h[:, h % 2, 0:T], ACT.Copy).then_inc(S["hi_ready"], 1)
            for f in range(4, KT):
                act.wait_ge(S["hn_ready"], 32 + f + 1)
                a(h_hi[:, f, REAL], n_h[:, f % 2, 0:T], ACT.Copy).then_inc(S["hi_ready"], 1)
            mixb = F2
            for f in range(KT):
                product(act, U_OUT2 + f)
                if f == 0:
                    act.wait_ge(S["h_ready"], 40)
                a(mixb[:, f, :], ps[:, f % 2, :], ACT.Copy)
                square(3, f, ps[:, f % 2, :], T)
            root(3, ps[:, 7, :], n_rs[:, 0:T])
            for f in range(KT):
                act.wait_ge(S["x_ready"], 16 + f + 1)
                square(4, f, xT[:, f, REAL], T)
            root(4, ps[:, 7, :], n_rs[:, 0:T])
            high(5, REAL)

            def up2(i):
                for q in range(4):
                    product(act, U_UP2 + q, i)
                    if isinstance(i, int):
                        wait(act, S["m2_ready"], 4 * i + q - 3)
                    else:
                        act.wait_ge(S["m2_ready"], 4 * i + (q - 3))
                    a(rb[:, q, :], ps[:, q, :], ACT.Relu).then_inc(S["relu_ready"], 1)

            rep(act, FT2 // 4, up2)
            us = U_DOWN2
            act.wait_ge(S["m2_ready"], FT2)
            rep(act, FT2 // 4, m_high(M2, 0, FT2))
            act.wait_ge(unit_done[(U_DOWN2 + 31) % 4], rounds(U_DOWN2 + 31))
            for f in range(KT):
                a(F2[:, f, :], ps[:, f, :], ACT.Copy).then_inc(S["f2_ready"], 1)
                square(5, f, ps[:, f, :], T)
            root(5, ps[:, 0, :], n_rs[:, 0:T])

        @block.tensor
        def _(pe):
            mm = nc.tensor.matmul

            def unit(u, i, work):
                pe.wait_ge(split_done[u % 4], rounds(u, i))
                last = work(w_hi[u % 4], w_lo[u % 4])
                last.then_inc(unit_done[u % 4], 1)

            def tile(u, i, dst, pieces=(REAL,)):
                def work(hi, lo):
                    for k in range(KT):
                        for n, (w, h) in enumerate(((hi, h_hi), (hi, h_lo), (lo, h_hi))):
                            for p, cols in enumerate(pieces):
                                last = mm(dst[p], w[:, k, :], h[:, k, cols], start=(k == 0 and n == 0),
                                          stop=(k == KT - 1 and n == 2))
                    return last
                unit(u, i, work)

            def squares(n, f, dst, cols):
                pe.wait_ge(S["sq_ready"], 8 * n + f + 1)
                for p, c in enumerate(cols):
                    last = mm(dst[p], ones[:], n_sq[:, f % 2, c], start=(f == 0), stop=(f == KT - 1))
                last.then_inc(S["sq_used"], 1)

            ALL = [slice(0, T)]
            pe.wait_ge(S["ones_ready"], 1)
            for f in range(KT):
                squares(0, f, [ps[:, 7, :]], ALL)
            pe.wait_ge(S["h_ready"], 8)
            for f in range(8):
                wait(pe, S["tile_read"], f - 1)
                tile(U_POOLIN + f, 0, [ps[:, f % 2, :]])

            def qk_side(t):
                pe.wait_ge(S["tile_read"], (9 if t == 0 else t + 10))
                wait(pe, S["qk_sqrt"], t - 1)
                wait(pe, S["qk_dve"], t - 1)
                mm(ps[:, 2 + t % 2, :], cst_ap("blk64"), sqb[:, t % 2, :], start=True, stop=True)
                mm(ps[:, 4 + t % 2, :], rot1, qgb[:, t % 2, :], start=True, stop=True).then_inc(S["qk_side"], 1)

            pe.wait_ge(S["tile_read"], 7)
            tile(U_KV, 0, [ps[:, 0, :]])
            pe.wait_ge(S["tile_read"], 8)
            tile(U_KV + 1, 0, [ps[:, 1, :]])
            pe.wait_ge(S["misc_loaded"], 48)
            qk_side(0)
            for t in range(1, 9):
                pe.wait_ge(S["tile_read"], t + 8)
                tile(U_Q + t - 1, 0, [ps[:, (9 + t) % 2, :]])
                if t == 1:
                    pe.wait_ge(S["qk_dve"], 1)
                    mm(ps[:, 6, :], cst_ap("swap"), KA, start=True, stop=True).then_inc(S["kb_done"], 1)
                    pe.wait_ge(S["rs_ready"], 1)
                    pe.wait_ge(S["tile_read"], 10)
                    for b in range(NB):
                        last = nc.tensor.transpose(ps[:, 7, b * P:(b + 1) * P], vT[:, b * P:(b + 1) * P], cst_ap("ident"))
                    last.then_inc(S["v_turned"], 1)
                if t > 1:
                    qk_side(t - 1)
            qk_side(8)

            def pooled(k):
                pe.wait_ge(S["win_ready"], 2 * k + 2)
                pe.wait_ge(S["pg_ready"], 2 * k + 2)

                def work(hi, lo):
                    for g in range(2):
                        for f in range(2):
                            for kk in range(2):
                                for n, (w, h) in enumerate(((hi, g_hi), (hi, g_lo), (lo, g_hi))):
                                    last = mm(ps[:, 2 + 2 * g + f, :], w[:, 4 * g + 2 * f + kk, :], h[:, 2 * g + kk, :],
                                              start=(kk == 0 and n == 0), stop=(kk == 1 and n == 2))
                    return last
                unit(U_PM + k, 0, work)

            def gate(i):
                pe.wait_ge(S["tile_read"], 18 + i - 1)
                tile(U_GATE + i, 0, [ps[:, i % 2, :]])

            pe.wait_ge(S["qk_dve"], 9)
            pooled(0)
            gate(0)
            gate(1)
            pe.wait_ge(S["pm_read"], 4)
            pooled(1)
            pe.wait_ge(S["pm_read"], 8)
            pe.wait_ge(S["kb_ready"], 1)
            pe.wait_ge(S["v_ready"], 1)

            def scores(n):
                blk, g, par = n // 4, n // 2 % 2, n % 2
                wait(pe, S["s_read"], n)
                K = KA if g == par else KB
                r = slice(64 * par, 64 * par + 64)
                c = slice((blk - 1) * P, (blk + 1) * P) if blk else slice(0, P)
                for m in range(4):
                    o = 256 * (m % 2) + (0 if blk else P)
                    last = mm(ps[:, 2 + m // 2, o:256 * (m % 2) + 256], Q[r, 4 * g + m, blk * P:(blk + 1) * P], K[r, c],
                              start=True, stop=True)
                last.then_inc(S["s_ready"], 1)

            def turn(n):
                blk = n // 4
                pe.wait_ge(S["p_ready"], n + 1)
                wait(pe, S["pT_copied"], n)
                for kb in range(0 if blk else 1, 2):
                    for m in range(4):
                        last = nc.tensor.transpose(ps[:, 4 + kb, m * P:(m + 1) * P], sm[n % 2][:, m, kb * P:(kb + 1) * P],
                                                   cst_ap("ident"))
                last.then_inc(S["pT_ready"], 1)

            def values(n):
                blk, g, par = n // 4, n // 2 % 2, n % 2
                pe.wait_ge(S["pT_copied"], n + 1)
                wait(pe, S["o_read"], n // 2 - 1)
                kbs = range(0 if blk else 1, 2)
                for kb in kbs:
                    last = mm(ps[64 * par:64 * par + 64, 6 + n // 2 % 2, :], vtok[:, blk - 1 + kb, 64 * g:64 * g + 64],
                              pT[:, kb, :], start=(kb == kbs[0]), stop=(kb == 1))
                last.then_inc(S["pv_done"], 1)

            scores(0)
            scores(1)
            for n in range(16):
                turn(n)
                if n < 14:
                    scores(n + 2)
                values(n)
                if n < 14:
                    gate(n + 2)
            pe.wait_ge(S["h_ready"], 16)
            pe.wait_ge(S["o_read"], 8)
            for f in range(KT):
                if f < 2:
                    pe.wait_ge(S["tile_read"], 34)
                else:
                    pe.wait_ge(S["x_ready"], f - 1)
                tile(U_OUT + f, 0, [ps[:, f % 2, :]])
                if f:
                    squares(1, f - 1, [ps[:, 7, :]], ALL)
            squares(1, 7, [ps[:, 7, :]], ALL)
            pe.wait_ge(S["h_ready"], 24)

            def up(i):
                for q in range(4):
                    if isinstance(i, int):
                        wait(pe, S["up_read"], 4 * i + q - 3)
                    else:
                        pe.wait_ge(S["up_read"], 4 * i + (q - 3))
                    tile(U_UP + q, i, [ps[:, q, :]])

            pe.wait_ge(S["x_ready"], 8)
            rep(pe, FT // 2, up)
            pe.wait_ge(S["up_read"], 2 * FT)

            def down(us, n0, i, j, start, stop):
                pe.wait_ge(S["ms_ready"], n0 + 4 * i + j + 1)

                def work(hi, lo):
                    for f in range(KT):
                        for n, (w, h) in enumerate(((hi, g_hi), (hi, g_lo), (lo, g_hi))):
                            last = mm(ps[:, f, :], w[:, f, :], h[:, j, :], start=(start and n == 0), stop=(stop and n == 2),
                                      skip_group_check=True)
                    return last
                unit(us + j, i, work)

            def down4(us, n0, first, final):
                def body(i):
                    for j in range(4):
                        down(us, n0, i, j, first and isinstance(i, int) and i == 0 and j == 0, final and j == 3)
                return body

            rep(pe, 5, down4(U_DOWN, 0, True, False))
            down(U_DOWN, 0, 5, 0, False, False)
            down(U_DOWN, 0, 5, 1, False, True)
            pe.wait_ge(S["x_ready"], 16)
            for f in range(KT):
                squares(2, f, [ps[:, 0, 0:HALF], ps[:, 1, 0:HALF]], halves)
            pe.wait_ge(S["rs_ready"], 3)
            pe.wait_ge(S["h_ready"], 32)

            def two(t):
                return [ps[:, 2 * (t % 2), 0:HALF], ps[:, 2 * (t % 2) + 1, 0:HALF]]

            def wide(n, u):
                wait(pe, S["t2_read"], n - 1)
                tile(u, 0, two(n), halves)

            def k2_side(t):
                pe.wait_ge(S["t2_read"], 1 if t == 0 else t + 2)
                wait(pe, S["k2_sqrt"], t)
                wait(pe, S["k2_dve"], t)
                if t == 1:
                    pe.wait_ge(S["kb2_ready"], 1)
                    pe.wait_ge(S["v2_ready"], 1)
                for c in range(2):
                    mm(ps[:, 4 + c, 0:HALF], cst_ap("blk64"), s5[:, halves[c]], start=True, stop=True)
                for c in range(2):
                    last = mm(ps[:, 6 + c, 0:HALF], cst_ap("rot2"), e5[:, halves[c]], start=True, stop=True)
                last.then_inc(S["k2_side"], 1)

            wide(0, U_AT2)
            wide(1, U_AT2 + 1)
            k2_side(0)
            wide(2, U_AT2 + 2)
            pe.wait_ge(S["k2_dve"], 1)
            pe.wait_ge(S["k2_sqrt"], 1)
            for c in range(2):
                last = mm(ps[:, 4 + c, 0:HALF], cst_ap("swap"), AKA[:, halves[c]], start=True, stop=True)
            last.then_inc(S["kb2_done"], 1)
            pe.wait_ge(S["t2_read"], 2)
            for b in range(5):
                c0 = META + P * b if b < 4 else 0
                last = nc.tensor.transpose(ps[:, 6 + b // 4, (b % 4) * P:(b % 4) * P + P], x5[:, 1, c0:c0 + P], cst_ap("ident"))
            last.then_inc(S["v2_turned"], 1)
            for t in range(1, 5):
                k2_side(t)
                if t < 4:
                    wide(2 + t, U_AT2 + 2 + t)

            pe.wait_ge(S["k2_dve"], 5)
            pe.wait_ge(S["ba_split"], 2)
            for b in range(5):
                c0 = META + P * b if b < 4 else 0
                for k in range(KT):
                    for n, (h, w) in enumerate(((h_hi, wba_hi), (h_hi, wba_lo), (h_lo, wba_hi))):
                        last = mm(ps[:, 7, 16 * b:16 * b + 16], h[:, k, c0:c0 + P], w[:, k, :],
                                  start=(k == 0 and n == 0), stop=(k == KT - 1 and n == 2))
            last.then_inc(S["ba_done"], 1)
            pe.wait_ge(S["ba_ready"], 3)
            for b in range(5):
                r = slice(0, P if b < 4 else META)
                for d in range(2):
                    mm(ps[:, 6, 8 * b + 4 * d:8 * b + 4 * d + 4], cst_ap("upto_b" if d and b < 4 else "upto_f")[r, :],
                       G[r, b, 4 * d:4 * d + 4], start=True, stop=True)
                last = mm(ps[:, 6, 40 + 8 * b:48 + 8 * b], ones[r, :], G[r, b, :], start=True, stop=True)
            last.then_inc(S["gc_done"], 1)
            pe.wait_ge(S["ba_ready"], 4)
            pe.wait_ge(S["tab_ready"], 3)

            def scores2(n):
                blk, h = n // 8, n % 8
                g, par = h // 4, h % 2
                wait(pe, S["e2_ready"], n)
                K = AKA if g == par else AKB
                r = slice(64 * par, 64 * par + 64)
                for c in range(2):
                    last = mm(ps[:, 4 + c, 0:HALF], AQ[r, h // 2, blk * P:(blk + 1) * P], K[r, halves[c]], start=True, stop=True)
                last.then_inc(S["s2_ready"], 1)

            def turn2(n):
                pe.wait_ge(S["p2_ready"], n + 1)
                wait(pe, S["pT2_copied"], n)
                wait(pe, S["o2_read"], n // 2)
                for b in range(5):
                    c0 = META + P * b if b < 4 else 0
                    last = nc.tensor.transpose(ps[:, 6 + b // 4, (b % 4) * P:(b % 4) * P + P],
                                               pp[n % 2][:, c0:c0 + P], cst_ap("ident"))
                last.then_inc(S["pT2_ready"], 1)

            def values2(n):
                h = n % 8
                g, par = h // 4, h % 2
                pe.wait_ge(S["pT2_copied"], n + 1)
                o = ps[64 * par:64 * par + 64, 7, 256:256 + P]
                for b in range(5):
                    r = slice(0, P if b < 4 else META)
                    last = mm(o, avtok[r, b, 64 * g:64 * g + 64], ppT[r, b, :], start=(b == 0), stop=(b == 4))
                last.then_inc(S["o2_done"], 1)

            def dn_sum(d):
                pe.wait_ge(S["dn_sq"], d + 1)
                for c in range(2):
                    last = mm(two(d)[c], ones[:], s5[:, halves[c]], start=True, stop=True)
                last.then_inc(S["dn_ss"], 1)

            def wide_half(d, part):
                u = U_DN2 + d
                if part == 0:
                    wait(pe, S["t2_read"], 6 + d - 1)
                    if d >= 2:
                        wait(pe, S["dn_sqrt"], min(d - 1, 8))
                    pe.wait_ge(split_done[u % 4], rounds(u))
                for k in range(4 * part, 4 * part + 4):
                    for n, (w, h) in enumerate(((w_hi, h_hi), (w_hi, h_lo), (w_lo, h_hi))):
                        for c in range(2):
                            last = mm(two(d)[c], w[u % 4][:, k, :], h[:, k, halves[c]], start=(k == 0 and n == 0),
                                      stop=(k == KT - 1 and n == 2))
                if part == 1:
                    last.then_inc(unit_done[u % 4], 1)

            scores2(0)
            wide_half(0, 0)
            scores2(1)
            wide_half(0, 1)
            for n in range(32):
                d = n // 2
                turn2(n)
                if n < 30:
                    scores2(n + 2)
                values2(n)
                if d < 15:
                    wide_half(d + 1, n % 2)
                if n % 2 and d < 8:
                    dn_sum(d)

            pe.wait_ge(S["dn_ready"], 8)
            pe.wait_ge(S["dn_c"], 16)
            pe.wait_ge(S["o2_read"], 16)
            for st in range(-1, NB):
                meta = st < 0
                w = META if meta else P
                r = slice(0, w)
                for name in PE_M if meta else PE_R:
                    for d in range(2):
                        b = lane[d]
                        L0, L1, L2, L3 = (ps[:, 4 * d + n, :] for n in range(4))
                        blk = 4 if meta else (3 - st if d else st)
                        c0 = 0 if meta else META + P * blk
                        cols = slice(c0, c0 + w)
                        U_ = cst_ap("upto_b" if d and not meta else "upto_f")
                        prev = pe_at(st, name) - 1

                        def hd(bank, h, w=w):
                            return bank[r, h * w:(h + 1) * w]

                        if name == "A":
                            wait(pe, dn_v[d], dve_at(st - 1, "O") if st > 0 else (dve_at(-1, "O") if st == 0 else 0))
                            for h in range(4):
                                gb = G[r, blk, 4 * d + h:4 * d + h + 1].to_broadcast([w, w])
                                bb = BETA[r, blk, 4 * d + h:4 * d + h + 1].to_broadcast([w, w])
                                mm(hd(L0, h) if meta else L0[:, h * P:(h + 1) * P], gb, U_[r, r], start=True, stop=True)
                                mm(hd(L1, h), bb, cst_ap("ident")[r, r], start=True, stop=True)
                                mm(hd(L2, h), DK[:, h, cols], DK[:, h, cols], start=True, stop=True)
                                last = mm(hd(L3, h), DK[:, h, cols], DQ[:, h, cols], start=True, stop=True)
                        elif name == "T":
                            pe.wait_ge(dn_v[d], dve_at(st, "E"))
                            for h in range(4):
                                if meta:
                                    last = mm(hd(L2, h), b["X"][r, h, r], cst_ap("ident")[r, r], start=True, stop=True)
                                else:
                                    last = nc.tensor.transpose(hd(L2, h), b["X"][:, h, :], cst_ap("ident"))
                        elif name[0] == "P":
                            n = int(name[1:])
                            pe.wait_ge(dn_v[d], dve_at(st, "X" if n == 1 else f"XY{n - 1}"))
                            if not meta:
                                pe.wait_ge(dn_p[d], NLEV * st + n)
                            pe.wait_ge(dn_a[d], act_at(st, "E" if n == 1 else f"P{n - 1}"))
                            for h in range(4):
                                last = mm(hd(L0, h), b["EM"][r, h, r], b["X"][r, h, r], start=True, stop=True)
                        elif name[:2] == "XY":
                            n = int(name[2:])
                            pe.wait_ge(dn_a[d], act_at(st, f"P{n}"))
                            final = n == (3 if meta else NLEV)
                            for h in range(4):
                                if not final:
                                    mm(hd(L1, h), b["Y"][r, h, r], b["P"][r, h, r], start=True, stop=True)
                                last = mm(hd(L2, h), b["P"][r, h, r], b["Y"][r, h, r], start=True, stop=True)
                        elif name == "KV":
                            pe.wait_ge(dn_v[d], dve_at(st, "XY3" if meta else "XY6"))
                            kc = slice(c0, c0 + P)
                            for h in range(4):
                                nc.tensor.transpose(L0[:, h * P:(h + 1) * P], DK[:, h, kc], cst_ap("ident"))
                                last = nc.tensor.transpose(L3[:, h * P:(h + 1) * P], DV[:, h, kc], cst_ap("ident"))
                        elif name == "KS":
                            for h in range(4):
                                last = mm(L1[:, h * P:(h + 1) * P], DK[:, h, cols], ST[d][:, h, :], start=True, stop=True)
                        elif name == "VN":
                            pe.wait_ge(dn_v[d], dve_at(st, "KV" if meta else "R"))
                            R = b["X"] if meta else b["P"]
                            for h in range(4):
                                last = mm(L2[r, h * P:(h + 1) * P], b["Y"][r, h, r], R[r, h, :], start=True, stop=True)
                        elif name == "OS":
                            pe.wait_ge(dn_a[d], act_at(st, "VN"))
                            for h in range(4):
                                hc = slice(h * P, (h + 1) * P)
                                if not meta:
                                    mm(L3[:, hc], ST[d][:, h, :], b["QE"][:, h, :], start=True, stop=False)
                                    mm(L3[:, hc], b["EM"][:, h, :], b["QD"][:, h, :], start=False, stop=True)
                                last = mm(L0[:, hc], b["AT"][r, h, :], b["EM"][r, h, :], start=True, stop=True)
                        last.then_inc(dn_pe[d], 1)

            for h in range(4):
                pe.wait_ge(S["on_sq"], h + 1)
                wait(pe, S["on_rs"], h - 1)
                mm(ps[:, h % 2, :], ones[:], n_sq[:, h % 2, 0:T], start=True, stop=True).then_inc(S["on_ss"], 1)
            pe.wait_ge(S["h_ready"], 40)
            pe.wait_ge(S["on_rs"], 4)
            for f in range(KT):
                wait(pe, S["sq_ready"], 24 + f - 1 if f > 1 else 0)
                tile(U_OUT2 + f, 0, [ps[:, f % 2, :]])
                if f:
                    squares(3, f - 1, [ps[:, 7, :]], ALL)
            squares(3, 7, [ps[:, 7, :]], ALL)
            pe.wait_ge(S["rs_ready"], 4)
            for f in range(KT):
                squares(4, f, [ps[:, 7, :]], ALL)
            pe.wait_ge(S["h_ready"], 48)

            def up2(i):
                for q in range(4):
                    if isinstance(i, int):
                        wait(pe, S["relu_ready"], 4 * i + q - 3)
                    else:
                        pe.wait_ge(S["relu_ready"], 4 * i + (q - 3))
                    tile(U_UP2 + q, i, [ps[:, q, :]])

            rep(pe, FT2 // 4, up2)
            pe.wait_ge(S["m2_ready"], FT2)
            rep(pe, FT2 // 4 - 1, down4(U_DOWN2, FT, True, False))
            for j in range(4):
                down(U_DOWN2, FT, FT2 // 4 - 1, j, False, j == 3)
            for f in range(KT):
                squares(5, f, [ps[:, 0, :]], ALL)

        @block.vector
        def _(dve):
            v = nc.vector
            step = Steps(dve, S["dve_step"])

            def inverse_root(n, w):
                dve.wait_ge(S["rs_ready"], n + 1)
                step(v.reciprocal(n_ri[:, 0:w], n_rs[:, 0:w]))
                step.settle()

            def parts(n, cols, normal):
                w = cols.stop - cols.start

                def low(f):
                    dve.wait_ge(S["hi_ready"], 8 * n + f + 1)
                    v.tensor_tensor(h_lo[:, f, cols], n_h[:, f % 2, 0:w], h_hi[:, f, cols], ALU.subtract).then_inc(S["h_ready"], 1)

                for f in range(KT):
                    if f >= 2:
                        dve.wait_ge(S["h_ready"], 8 * n + f - 1)
                    normal(f, n_h[:, f % 2, 0:w])
                    if f:
                        low(f - 1)
                low(KT - 1)

            def gained(name, cols):
                w = cols.stop - cols.start

                def normal(f, dst):
                    v.scalar_tensor_tensor(out=dst, in0=xT[:, f, cols], scalar=vcol(name, f), in1=n_ri[:, 0:w],
                                           op0=ALU.mult, op1=ALU.mult).then_inc(S["hn_ready"], 1)
                return normal

            v.memset(ones[:], 1.0).then_inc(S["ones_ready"], 1)
            v.memset(U[:, :, 0:META], 0.0)
            dve.wait_ge(S["v_loaded"], 16)
            for name, n, c in (("q_norm", 1, 0.125), ("q_norm2", 1, 0.125), ("b_gate", 16, 0.5), ("pool_scale", 8, 0.5),
                               ("dn_norm", 1, 0.5)):
                x = V[:, VOFF[name]:VOFF[name] + n]
                step(v.tensor_scalar(x, x, c, None, ALU.mult))
            dve.wait_ge(S["misc_loaded"], 48)
            step(v.tensor_copy(posf, posi))
            step.settle()
            step(v.tensor_scalar(ang, posf, invf, None, ALU.mult))
            step.settle()
            big = 12582912.0
            step(v.tensor_scalar(ab, ang, 1.0 / (2 * np.pi), None, ALU.mult))
            step.settle()
            step(v.tensor_scalar(ab, ab, big, None, ALU.add))
            step.settle()
            step(v.tensor_scalar(ab, ab, big, None, ALU.subtract))
            step.settle()
            src = ang
            for c, dst in ((6.28125, nrd), (0.0019340515136718750, ang), (1.2556659146e-06, nrd)):
                step(v.scalar_tensor_tensor(out=dst, in0=ab, scalar=-c, in1=src, op0=ALU.mult, op1=ALU.add))
                step.settle()
                src = dst
            v.tensor_scalar(nrd, nrd, 3.1415925, -3.1415925, ALU.min, ALU.max).then_inc(S["rope_ready"], 1)
            dve.wait_ge(S["rope_ready"], 1)
            step(v.tensor_scalar(ang, nrd, -1.0, None, ALU.mult))
            step.settle()
            v.tensor_tensor(ab, nrd, ang, ALU.max).then_inc(S["rope_ready"], 1)

            inverse_root(0, T)
            parts(0, REAL, gained("attn_norm", REAL))

            def windows(g):
                u2 = U[:, 2 * g:2 * g + 2, :]
                dve.wait_ge(S["tile_read"], 2 * g + 2)
                wait(dve, S["win_ready"], g)
                src, d = u2, 1
                for n in range(g + 1):
                    dst = (W0, W1)[n % 2]
                    lo = 2 * d - 1
                    step(v.tensor_tensor(dst[:, :, lo:L], src[:, :, lo:L], src[:, :, lo - d:L - d], ALU.add))
                    step.settle()
                    src, d = dst, 2 * d
                other = W1 if src is W0 else W0
                cnt = cnt16[:, 16 * g:16 * g + 16].unsqueeze(1).to_broadcast([P, 2, 16])
                step(v.tensor_tensor(other[:, :, 0:16], src[:, :, META:META + 16], cnt, ALU.mult))
                step.settle()
                step(v.tensor_tensor(u2[:, :, META:META + 16], other[:, :, 0:16], u2[:, :, META:META + 16], ALU.subtract))
                v.scalar_tensor_tensor(out=u2[:, :, META + 16:L], in0=src[:, :, META + 16:L], scalar=1.0 / d,
                                       in1=u2[:, :, META + 16:L], op0=ALU.mult, op1=ALU.subtract).then_inc(S["win_ready"], 1)

            def window_parts(g):
                dve.wait_ge(S["win_ready"], g + 1)
                if g >= 2:
                    product(dve, U_PM)
                s = slice(2 * (g % 2), 2 * (g % 2) + 2)
                x = U[:, 2 * g:2 * g + 2, REAL]
                step(v.tensor_copy(g_hi[:, s, :], x))
                step.settle()
                v.tensor_tensor(g_lo[:, s, :], x, g_hi[:, s, :], ALU.subtract).then_inc(S["pg_ready"], 1)

            def qk(t):
                out_ = KA if t == 0 else Q[:, t - 1, :]
                dve.wait_ge(S["qk_sqrt"], t + 1)
                if t == 0:
                    dve.wait_ge(S["rope_ready"], 4)
                wait(dve, S["qk_dve"], t)
                step(v.reciprocal(rinv, rs[:, t % 2, :]))
                step(v.tensor_tensor(t1, qgb[:, t % 2, :], rope_c, ALU.mult))
                step(v.tensor_tensor(t2, ps[:, 4 + t % 2, :], rope_s, ALU.mult))
                step.settle()
                step(v.tensor_tensor(t1, t1, t2, ALU.add))
                step.settle()
                v.tensor_tensor(out_, t1, rinv, ALU.mult).then_inc(S["qk_dve"], 1)

            step(v.reciprocal(cnt16, cnt16))
            step.settle()
            windows(0)
            qk(0)
            window_parts(0)
            qk(1)
            windows(1)
            qk(2)
            window_parts(1)
            qk(3)
            windows(2)
            qk(4)
            qk(5)
            windows(3)
            qk(6)
            qk(7)
            qk(8)
            window_parts(2)
            window_parts(3)

            def masked_max(n):
                b = 16 * (n % 2)
                lo = 0 if n >= 4 else P
                s = sm[n % 2][:, :, lo:256]
                dve.wait_ge(S["s_ready"], n + 1)
                wait(dve, S["pT_ready"], n - 1)
                m = band[:, lo:256].unsqueeze(1).to_broadcast([P, 4, 256 - lo])
                v.tensor_tensor(s, ps[:, 2:4, :].rearrange("p a (b c) -> p (a b) c", c=256)[:, :, lo:256], m, ALU.add
                                ).then_inc(S["s_read"], 1)
                dve.wait_ge(S["s_read"], n + 1)
                step(v.tensor_reduce(small[:, b + 8:b + 12], s, AX, ALU.max))
                step.settle()
                hs = V[:, VOFF["sinks"] + 4 * (n % 4):VOFF["sinks"] + 4 * (n % 4) + 4]
                step(v.tensor_tensor(small[:, b + 8:b + 12], small[:, b + 8:b + 12], hs, ALU.max))
                step.settle()
                step(v.tensor_scalar(small[:, b:b + 4], small[:, b + 8:b + 12], -1.0, None, ALU.mult))
                step.settle()
                v.tensor_tensor(small[:, b + 4:b + 8], small[:, b:b + 4], hs, ALU.add).then_inc(S["mx_ready"], 1)

            def normalise(n):
                b = 16 * (n % 2)
                lo = 0 if n >= 4 else P
                s = sm[n % 2][:, :, lo:256]
                dve.wait_ge(S["exp_ready"], n + 1)
                den = small[:, b + 8:b + 12]
                step(v.tensor_tensor(den, den, small[:, b + 12:b + 16], ALU.add))
                step.settle()
                step(v.reciprocal(den, den))
                step.settle()
                v.tensor_tensor(s, s, den.unsqueeze(2).to_broadcast([P, 4, 256 - lo]), ALU.mult).then_inc(S["p_ready"], 1)

            def gate_pool(i):
                dve.wait_ge(S["tile_read"], 26 + i + 1)
                dve.wait_ge(S["pm_read"], 8)
                v.scalar_tensor_tensor(out=U[:, i, REAL], in0=tg[:, i % 2, :], scalar=1.0, in1=U[:, i, REAL],
                                       op0=ALU.add, op1=ALU.mult).then_inc(S["gp_done"], 1)

            def attn_out(n):
                blk, g = n // 4, n // 2 % 2
                dve.wait_ge(S["pv_done"], n + 1)
                v.tensor_copy(Q[:, 4 * g:4 * g + 4, blk * P:(blk + 1) * P],
                              ps[:, 6 + n // 2 % 2, :].rearrange("p (a b) -> p a b", b=P)).then_inc(S["o_read"], 1)

            masked_max(0)
            masked_max(1)
            normalise(0)
            for n in range(16):
                if n < 14:
                    masked_max(n + 2)
                if n < 15:
                    normalise(n + 1)
                if n % 2:
                    attn_out(n)
                if 7 <= n < 15:
                    gate_pool(n - 7)

            def mixed(f, dst):
                if f == 0:
                    dve.wait_ge(S["gp_done"], 8)
                    dve.wait_ge(S["o_read"], 8)
                    dve.wait_ge(S["tile_read"], 34)
                step(v.scalar_tensor_tensor(out=GA[:, f, :], in0=GA[:, f, :], scalar=1.0, in1=Q[:, f, :], op0=ALU.add, op1=ALU.mult))
                step.settle()
                v.scalar_tensor_tensor(out=dst, in0=GA[:, f, :], scalar=0.5, in1=U[:, f, REAL], op0=ALU.mult, op1=ALU.add
                                       ).then_inc(S["hn_ready"], 1)

            parts(1, REAL, mixed)
            for f in range(KT):
                product(dve, U_OUT + f)
                v.tensor_tensor(xT[:, f, REAL], xT[:, f, REAL], ps[:, f % 2, :], ALU.add).then_inc(S["x_ready"], 1)
            inverse_root(1, T)
            parts(2, REAL, gained("ffn_norm", REAL))

            def up(i):
                for h in range(2):
                    j = 2 * i + h
                    for e, dst in ((0, cg), (1, cv)):
                        q = 2 * h + e
                        w = VOFF["conv_w"] + e * FT
                        dve.wait_ge(S["up_act"], 4 * i + q + 1)
                        v.scalar_tensor_tensor(out=dst[:, h, 1:T], in0=ps[:, q, 0:T - 1], scalar=V[:, ds(j + (w + 2 * FT))],
                                               in1=dst[:, h, 1:T], op0=ALU.mult, op1=ALU.add).then_inc(S["dve_up"], 1)
                        dve.wait_ge(S["dve_up"], 4 * i + q + 1)
                        v.scalar_tensor_tensor(out=dst[:, h, 2:T], in0=ps[:, q, 0:T - 2], scalar=V[:, ds(j + w)],
                                               in1=dst[:, h, 2:T], op0=ALU.mult, op1=ALU.add).then_inc(S["up_read"], 1)
                    dve.wait_ge(S["up_read"], 4 * i + 2 * h + 2)
                    dve.wait_ge(S["silu_ready"], 2 * i + h + 1)
                    v.tensor_tensor(M1[:, ds(j), :].rearrange("p a b -> p (a b)"), eg[:, h, :], cv[:, h, :], ALU.mult
                                    ).then_inc(S["m1_ready"], 1)

            rep(dve, FT // 2, up)

            def m_low(src, n0, j, i):
                dve.wait_ge(S["ms_hi"], n0 + 4 * i + j + 1)
                v.tensor_tensor(g_lo[:, j, :], src[:, ds(4 * i + j), :].rearrange("p a b -> p (a b)"), g_hi[:, j, :],
                                ALU.subtract).then_inc(S["ms_ready"], 1)

            def low4(src, n0):
                def body(i):
                    for j in range(4):
                        m_low(src, n0, j, i)
                return body

            dve.wait_ge(S["m1_ready"], FT)
            rep(dve, 5, low4(M1, 0))
            m_low(M1, 0, 0, 5)
            m_low(M1, 0, 1, 5)
            product(dve, U_DOWN + FT - 1)
            for f in range(KT):
                v.tensor_tensor(xT[:, f, REAL], xT[:, f, REAL], ps[:, f, :], ALU.add).then_inc(S["x_ready"], 1)
            inverse_root(2, L)
            parts(3, slice(0, L), gained("mix_pre", slice(0, L)))

            dve.wait_ge(S["ba_split"], 1)
            v.tensor_tensor(wba_lo[:], wba32, wba_hi[:], ALU.subtract).then_inc(S["ba_split"], 1)

            def flat(x):
                return x.rearrange("p (a b) -> p a b", a=2)

            dve.wait_ge(S["c2_loaded"], 16)
            for t in range(5):
                dve.wait_ge(S["k2_sqrt"], t + 1)
                if t == 1:
                    dve.wait_ge(S["v2_turned"], 1)
                wait(dve, S["k2_dve"], t)
                step(v.reciprocal(i5, r5))
                step(v.tensor_tensor(y5, e5, c2, ALU.mult))
                step(v.tensor_tensor(flat(x5[:, 0, 0:L]), ps[:, 6:8, 0:HALF], flat(s2), ALU.mult))
                step.settle()
                step(v.tensor_tensor(y5, y5, x5[:, 0, 0:L], ALU.add))
                step.settle()
                if t == 0:
                    v.tensor_tensor(AKA, y5, i5, ALU.mult).then_inc(S["k2_dve"], 1)
                else:
                    v.tensor_tensor(AQ[:, t - 1, :], y5[:, REAL], i5[:, REAL], ALU.mult).then_inc(S["k2_dve"], 1)
            v.memset(x5[:, :, 0:2], 0.0)
            v.memset(x5[:, :, L + 2:L + 4], 0.0).then_inc(S["pads_ready"], 1)

            dve.wait_ge(S["ba_done"], 1)
            a_ps = ps[:, 7, 0:80].rearrange("p (a b) -> p a b", b=16)[:, :, 8:16]

            def row(name):
                return V[:, VOFF[name]:VOFF[name] + 8].unsqueeze(1).to_broadcast([P, 5, 8])

            step(v.tensor_tensor(tb[1], a_ps, row("dt_bias"), ALU.add))
            step.settle()
            step(v.tensor_scalar(tb[2], tb[1], -1.0, None, ALU.mult))
            step.settle()
            v.tensor_tensor(tb[2], tb[2], tb[1], ALU.max).then_inc(S["ba_ready"], 1)
            dve.wait_ge(S["tab_ready"], 1)
            v.tensor_scalar(tb[3], tb[2], 1.0, None, ALU.add).then_inc(S["ba_ready"], 1)
            dve.wait_ge(S["ba_ready"], 2)
            step(v.tensor_scalar(GCC, tb[3], 1.0, None, ALU.subtract))
            step.settle()
            step(v.tensor_tensor(GCC, tb[2], GCC, ALU.subtract))
            step.settle()
            step(v.reciprocal(tb[2], tb[3]))
            step(v.tensor_scalar(tb[1], tb[1], 0.0, None, ALU.max))
            step.settle()
            step(v.tensor_tensor(GCC, GCC, tb[2], ALU.mult))
            step.settle()
            step(v.tensor_tensor(GCC, GCC, tb[1], ALU.add))
            step.settle()
            dve.wait_ge(S["tab_ready"], 2)
            step(v.tensor_tensor(GCC, GCC, NBE, ALU.add))
            step.settle()
            v.scalar_tensor_tensor(out=G, in0=GCC, scalar=-1.0, in1=small2[:, 8:16].unsqueeze(1).to_broadcast([P, 5, 8]),
                                   op0=ALU.mult, op1=ALU.mult).then_inc(S["ba_ready"], 1)
            step(v.tensor_scalar(BETA, tb[0], 0.5, 0.5, ALU.mult, ALU.add))
            step.settle()
            step(v.tensor_scalar(BH, BETA, 0.5, None, ALU.mult))
            dve.wait_ge(S["gc_done"], 1)
            step(v.tensor_copy(GCC, ps[:, 6, 0:40].rearrange("p (a b) -> p a b", b=8)))
            step.settle()
            v.tensor_tensor(KD, ps[:, 6, 40:80].rearrange("p (a b) -> p a b", b=8), GCC, ALU.subtract).then_inc(S["ba_ready"], 1)
            dve.wait_ge(S["tab_ready"], 3)
            step(v.scalar_tensor_tensor(out=NBE, in0=tb[1], scalar=-1.0, in1=BETA, op0=ALU.mult, op1=ALU.mult))
            step.settle()

            def max2(n):
                dve.wait_ge(S["s2_ready"], n + 1)
                v.tensor_reduce(small2[:, n % 2:n % 2 + 1], ps[:, 4:6, 0:HALF], mybir.AxisListType.XY, ALU.max, negate=True
                                ).then_inc(S["mx2_ready"], 1)

            def norm2(n):
                rs2 = small2[:, 2 + n % 2:3 + n % 2]
                dve.wait_ge(S["e2_ready"], n + 1)
                step(v.reciprocal(rs2, rs2))
                step.settle()
                v.tensor_scalar(pp[n % 2][:, 0:L], pp[n % 2][:, 0:L], rs2, None, ALU.mult).then_inc(S["p2_ready"], 1)

            def out2(n):
                if n % 2:
                    dve.wait_ge(S["o2_done"], n + 1)
                    blk, h = n // 8, n % 8
                    v.tensor_copy(AQ[:, h // 2, blk * P:(blk + 1) * P], ps[:, 7, 256:256 + P]).then_inc(S["o2_read"], 1)

            def conv(d):
                dve.wait_ge(S["c_act"], 2 * d + 1)
                dve.wait_ge(S["pads_ready"], 1)
                for n, j in enumerate((0, 1, 3, 4)):
                    ins = v.scalar_tensor_tensor(out=y5, in0=x5[:, d % 2, j:j + L], scalar=vcol("dconv", 12 * j + d), in1=y5,
                                                 op0=ALU.mult, op1=ALU.add)
                    if n < 3:
                        step(ins)
                        step.settle()
                    else:
                        ins.then_inc(S["dn_dve"], 1)

            def silu(d):
                if d < 12:
                    dve.wait_ge(S["dn_dve"], d + 1)
                    dve.wait_ge(S["c_act"], 2 * d + 2)
                    v.scalar_tensor_tensor(out=(DQ, DK, DV)[d // 4][:, d % 4, :], in0=e5, scalar=1.0, in1=y5, op0=ALU.add,
                                           op1=ALU.mult).then_inc(S["dn_c"], 1)
                else:
                    dve.wait_ge(S["c_act"], 24 + d - 12 + 1)
                    v.scalar_tensor_tensor(out=DZ[:, d - 12, :], in0=e5[:, 0:T], scalar=1.0, in1=x5[:, d % 2, 2 + META:2 + L],
                                           op0=ALU.add, op1=ALU.mult).then_inc(S["dn_c"], 1)

            def conv_norm(d):
                dst = (DQ if d < 4 else DK)[:, d % 4, :]
                dve.wait_ge(S["dn_sqrt"], d + 1)
                step(v.reciprocal(i5, r5))
                step.settle()
                v.tensor_tensor(dst, dst, i5, ALU.mult).then_inc(S["dn_ready"], 1)

            for n in range(2):
                max2(n)
                norm2(n)
            for n in range(32):
                d = n // 2
                if n < 30:
                    max2(n + 2)
                if n % 2 == 0 and d < 12:
                    conv(d)
                out2(n)
                if n < 30:
                    norm2(n + 2)
                if n % 2:
                    silu(d)
                    if 1 <= d <= 8:
                        conv_norm(d - 1)

            for st in range(-1, NB):
                meta = st < 0
                w = META if meta else P
                r = slice(0, w)
                for name in DVE_M if meta else DVE_R:
                    for d in range(2):
                        b = lane[d]
                        L0, L1, L2, L3 = (ps[:, 4 * d + n, :].rearrange("p (a b) -> p a b", b=P) for n in range(4))
                        if meta:
                            S0, S1, S2, S3 = (ps[r, 4 * d + n, 0:4 * w].rearrange("p (a b) -> p a b", b=w) for n in range(4))
                        else:
                            S0, S1, S2, S3 = L0, L1, L2, L3
                        blk = 4 if meta else (3 - st if d else st)
                        c0 = META + P * blk
                        EM, X, Y, AT = (b[n][r, :, r] for n in ("EM", "X", "Y", "AT"))
                        U_ = cst_ap("upto_b" if d and not meta else "upto_f")[r, r].unsqueeze(1).to_broadcast([w, 4, w])
                        eye = cst_ap("ident")[r, r].unsqueeze(1).to_broadcast([w, 4, w])

                        def level(n):
                            m = cst_ap("lev_b" if d and not meta else "lev_f", P, P * n)
                            return m[r, r].unsqueeze(1).to_broadcast([w, 4, w])

                        def col(t, w2):
                            return t[r, blk, 4 * d:4 * d + 4].unsqueeze(2).to_broadcast([w, 4, w2])

                        if name == "D":
                            dve.wait_ge(dn_pe[d], pe_at(st, "A"))
                            step(v.tensor_tensor(EM, S0, col(GCC, w), ALU.subtract))
                            step.settle()
                            last = v.tensor_scalar(EM, EM, 0.0, None, ALU.min)
                        elif name == "E":
                            dve.wait_ge(dn_a[d], act_at(st, "E"))
                            step(v.tensor_tensor(EM, EM, U_, ALU.mult))
                            if not meta:
                                step(v.tensor_tensor(b["QE"], b["QE"], DQ[:, :, c0:c0 + P], ALU.mult))
                            step.settle()
                            if not meta:
                                step(v.tensor_tensor(b["QD"], S3, EM, ALU.mult))
                            step(v.tensor_tensor(AT, S2, EM, ALU.mult))
                            step.settle()
                            step(v.tensor_tensor(AT, AT, S1, ALU.mult))
                            step.settle()
                            step(v.tensor_tensor(X, AT, level(0), ALU.mult))
                            step.settle()
                            last = v.tensor_tensor(Y, eye, X, ALU.subtract)
                        elif name == "X":
                            dve.wait_ge(dn_pe[d], pe_at(st, "T"))
                            if meta:
                                step(v.tensor_tensor(EM, AT, level(1), ALU.mult))
                            last = v.tensor_tensor(X, eye, S2, ALU.subtract)
                        elif name[:2] == "XY":
                            n = int(name[2:])
                            dve.wait_ge(dn_pe[d], pe_at(st, name))
                            if n < (3 if meta else NLEV):
                                step(v.tensor_tensor(X, X, S1, ALU.subtract))
                                if meta:
                                    step(v.tensor_tensor(EM, AT, level(n + 1), ALU.mult))
                            last = v.tensor_tensor(Y, Y, S2, ALU.subtract)
                        elif name == "KV":
                            dve.wait_ge(dn_pe[d], pe_at(st, "KV"))
                            if not meta:
                                dve.wait_ge(dn_p[d], NLEV * (st + 1))
                            step(v.tensor_tensor(b["AT"][r], L0[r], col(KD, P), ALU.mult))
                            last = v.tensor_tensor(b["X"][r], L3[r], col(BH, P), ALU.mult)
                        elif name == "R":
                            dve.wait_ge(dn_pe[d], pe_at(st, "KS"))
                            dve.wait_ge(dn_v[d], dve_at(st, "KV"))
                            step(v.tensor_tensor(b["P"], L1, col(NBE, P), ALU.mult))
                            step.settle()
                            last = v.tensor_tensor(b["P"], b["P"], b["X"], ALU.add)
                        elif name == "O":
                            dve.wait_ge(dn_pe[d], pe_at(st, "OS"))
                            if meta:
                                last = v.tensor_copy(ST[d], L0)
                            else:
                                o = OD[:, :, blk * P:(blk + 1) * P]
                                if st < 2:
                                    step(v.tensor_copy(o, L3))
                                else:
                                    step(v.tensor_tensor(o, o, L3, ALU.add))
                                egl = EGL[:, blk, 4 * d:4 * d + 4].unsqueeze(2).to_broadcast([P, 4, P])
                                step(v.tensor_tensor(ST[d], ST[d], egl, ALU.mult))
                                step.settle()
                                last = v.tensor_tensor(ST[d], ST[d], L0, ALU.add)
                        last.then_inc(dn_v[d], 1)

            def heads(f, dst):
                if f < 4:
                    dve.wait_ge(S["on_rs"], f + 1)
                    wait(dve, S["hn_ready"], 32 + f)
                    step(v.reciprocal(n_ri[:, 0:T], n_rs[:, 0:T]))
                    step.settle()
                    step(v.scalar_tensor_tensor(out=OD[:, f, :], in0=OD[:, f, :], scalar=vcol("dn_norm"), in1=n_ri[:, 0:T],
                                                op0=ALU.mult, op1=ALU.mult))
                    step.settle()
                    v.tensor_tensor(dst, OD[:, f, :], DZ[:, f, :], ALU.mult).then_inc(S["hn_ready"], 1)
                else:
                    v.tensor_copy(dst, AQ[:, f - 4, :]).then_inc(S["hn_ready"], 1)

            parts(4, REAL, heads)
            mixb = F2

            def add_normed(src, name, f):
                step(v.scalar_tensor_tensor(out=src[:, f, :], in0=src[:, f, :], scalar=vcol(name, f), in1=n_ri[:, 0:T],
                                            op0=ALU.mult, op1=ALU.mult))
                step.settle()
                v.tensor_tensor(xT[:, f, REAL], xT[:, f, REAL], src[:, f, :], ALU.add).then_inc(S["x_ready"], 1)

            inverse_root(3, T)
            for f in range(KT):
                add_normed(mixb, "mix_post", f)
            inverse_root(4, T)
            parts(5, REAL, gained("mlp_pre", REAL))

            def up2(i):
                for q in range(4):
                    dve.wait_ge(S["relu_ready"], 4 * i + q + 1)
                    v.tensor_tensor(M2[:, ds(4 * i + q), :].rearrange("p a b -> p (a b)"), rb[:, q, :], rb[:, q, :], ALU.mult
                                    ).then_inc(S["m2_ready"], 1)

            rep(dve, FT2 // 4, up2)
            dve.wait_ge(S["m2_ready"], FT2)
            rep(dve, FT2 // 4, low4(M2, FT))
            inverse_root(5, T)
            for f in range(KT):
                add_normed(F2, "mlp_post", f)


def _tiles(w):
    k, n = w.shape
    return w.reshape(k // P, P, n // P, P).transpose(2, 1, 0, 3).reshape(n // P, P, k)


def _cols(v):
    return np.ascontiguousarray(np.asarray(v).reshape(-1, P).T)


def kernel(**inputs):
    import concourse.bacc as _bacc
    from concourse.bass_utils import run_bass_kernel_spmd as _run

    I = {k: np.asarray(v) for k, v in inputs.items()}
    w_in, w_up, w_in2 = I["w_in"][0], I["w_up"][0], I["w_in_2"][0]
    t_in = _tiles(w_in)
    t_up = np.stack([_tiles(w_up[:, :FF]), _tiles(w_up[:, FF:])], 1).reshape(2 * FT, P, D)
    pool = I["w_pool"][0].reshape(2, 2, 2, P, 2, P).transpose(0, 3, 1, 4, 2, 5).reshape(2, P, D)
    t_at = _tiles(w_in2[:, 2064:2832])
    stream = np.concatenate([
        t_in[0:8], t_in[16:18], t_in[8:16], pool, t_in[26:34], t_in[18:26], _tiles(I["w_out"][0]), t_up,
        I["w_down"][0].reshape(FT, P, D), t_at[4:6], t_at[0:4], _tiles(w_in2[:, 0:2048]), _tiles(I["w_out_2"][0]),
        _tiles(I["w_up_2"][0]), I["w_down_2"][0].reshape(FT2, P, D)])
    w_ba = np.ascontiguousarray(w_in2[:, 2048:2064].reshape(KT, P, 16).transpose(1, 0, 2).reshape(P, KT * 16))
    x = np.concatenate([I["meta_tokens_2"], I["x"][0]])
    x_t = np.ascontiguousarray(x.T.reshape(KT, P, L).transpose(1, 0, 2))

    def rows(v):
        return np.broadcast_to(np.asarray(v).reshape(1, -1), (P, np.asarray(v).size))

    def twice(v):
        return np.concatenate([v[0], v[0]]).reshape(P, 1)

    sinks = I["sinks"][0].reshape(2, 4, 2).transpose(0, 2, 1)
    vec = np.ascontiguousarray(np.concatenate([
        _cols(I["attn_norm"]), _cols(I["b_gate"]), _cols(I["pool_scale"]), twice(I["q_norm"]), twice(I["k_norm"]),
        rows(sinks), _cols(I["ffn_norm"]), _cols(I["conv_w"]), _cols(I["conv_b"]), _cols(I["norm_mix_pre_2"]),
        _cols(I["norm_mix_post_2"]), _cols(I["norm_mlp_pre_2"]), _cols(I["norm_mlp_post_2"]), _cols(I["conv_w_2"]),
        rows(I["a_log_2"]), rows(I["dt_bias_2"]), I["dn_out_norm_2"].reshape(P, 1), twice(I["q_norm_2"]),
        twice(I["k_norm_2"])], 1))
    cst, cst1, cst2 = constants()
    pos = np.ascontiguousarray(np.broadcast_to(I["positions"].reshape(1, T), (P, T)))
    arrays = {"w_stream": stream, "w_ba": w_ba.reshape(P, KT, 16), "x_t": x_t, "vec": vec, "cst": cst, "cst1": cst1, "cst2": cst2,
              "pos": pos}
    nc = _bacc.Bacc("TRN2", target_bir_lowering=False, num_devices=1)
    args = [nc.dram_tensor(f"in_{n}", a.shape, mybir.dt.from_np(a.dtype), kind="ExternalInput").ap() for n, a in arrays.items()]
    out = nc.dram_tensor("out_0", (P, KT, T), F32, kind="ExternalOutput").ap()
    build(nc, *args, out)
    r = _run(nc, [{f"in_{n}": a for n, a in arrays.items()}], core_ids=[0])
    return r.results[0]["out_0"].transpose(2, 1, 0).reshape(1, T, D)
```
